# Optimizing a Trainium2 kernel written in Bass

```python
import jax, jax.numpy as jnp
from jax import lax
import numpy as np

D_MODEL = 1024
BATCH = 1
SEQ = 1024
DEPTH = 1

GLA_HEADS = 4
GLA_DK = D_MODEL // 2 // GLA_HEADS
GLA_DV = D_MODEL // GLA_HEADS
GLA_RANK = 16
GLA_TAU = 16.0
GLA_CHUNK = 64
CONV_WIDTH = D_MODEL
CONV_K = 3
N_EXPERTS = 32
TOP_K = 4
D_FF = D_MODEL
SWIGLU_LIMIT = 7.0
SWIGLU_ALPHA = 1.702
EPS = 1e-6

QK_W = GLA_HEADS * GLA_DK
V_W = GLA_HEADS * GLA_DV
SPLITS = (QK_W, QK_W, V_W, V_W, GLA_RANK, CONV_WIDTH, CONV_WIDTH, CONV_WIDTH, D_MODEL, D_MODEL)
IN_PROJ_W = sum(SPLITS)

kernel_name = "hybrid_gla_shortconv_moe_block"

def rms_norm(x, g):
    xf = x.astype(jnp.float32)
    y = xf * lax.rsqrt(jnp.mean(xf * xf, axis=-1, keepdims=True) + EPS)
    return (y * g.astype(jnp.float32)).astype(x.dtype)

def split_columns(z):
    offsets = [int(o) for o in np.cumsum(SPLITS)[:-1]]
    return jnp.split(z, offsets, axis=-1)

def gla_chunked(q, k, v, log_a):
    B, S, H, DK = q.shape
    DV = v.shape[-1]
    C = GLA_CHUNK
    N = S // C
    f32 = jnp.float32
    qf = q.astype(f32).reshape(B, N, C, H, DK) * (DK ** -0.5)
    kf = k.astype(f32).reshape(B, N, C, H, DK)
    vf = v.astype(f32).reshape(B, N, C, H, DV)
    b = jnp.cumsum(log_a.astype(f32).reshape(B, N, C, H, DK), axis=2)
    b_last = b[:, :, -1]
    q_dec = qf * jnp.exp(b)
    k_inv = kf * jnp.exp(-b)
    k_tail = kf * jnp.exp(b_last[:, :, None] - b)
    scores = jnp.einsum("bnihd,bnjhd->bnhij", q_dec, k_inv)
    causal = jnp.tril(jnp.ones((C, C), dtype=bool))
    scores = jnp.where(causal, scores, 0.0)
    o_intra = jnp.einsum("bnhij,bnjhv->bnihv", scores, vf)
    chunk_update = jnp.einsum("bnjhd,bnjhv->nbhdv", k_tail, vf)
    chunk_decay = jnp.exp(b_last).transpose(1, 0, 2, 3)

    def step(state, inp):
        dec, upd = inp
        return dec[..., None] * state + upd, state

    state0 = jnp.zeros((B, H, DK, DV), f32)
    _, state_in = lax.scan(step, state0, (chunk_decay, chunk_update))
    o_inter = jnp.einsum("bnihd,nbhdv->bnihv", q_dec, state_in)
    return (o_intra + o_inter).reshape(B, S, H, DV).astype(v.dtype)

def causal_dwconv(u, w):
    S = u.shape[1]
    up = jnp.pad(u, ((0, 0), (CONV_K - 1, 0), (0, 0)))
    y = w[0] * up[:, 0:S]
    for i in range(1, CONV_K):
        y = y + w[i] * up[:, i:i + S]
    return y

def moe_ffn(h, w_router, b_router, w_gate_up, b_gate_up, w_down, b_down):
    B, S, D = h.shape
    T = B * S
    xt = h.reshape(T, D)
    logits = jnp.matmul(xt, w_router).astype(jnp.float32) + b_router.astype(jnp.float32)
    top_logit, top_idx = lax.top_k(logits, TOP_K)
    gates = jax.nn.softmax(top_logit, axis=-1)
    flat_e = top_idx.reshape(-1)
    order = jnp.argsort(flat_e)
    e_sorted = flat_e[order]
    tok_sorted = order // TOP_K
    group_sizes = jnp.bincount(flat_e, length=N_EXPERTS).astype(jnp.int32)
    xs = xt[tok_sorted]
    gu = lax.ragged_dot(xs, w_gate_up, group_sizes) + b_gate_up[e_sorted]
    gate, lin = jnp.split(gu, 2, axis=-1)
    gate = jnp.minimum(gate, SWIGLU_LIMIT)
    lin = jnp.clip(lin, -SWIGLU_LIMIT, SWIGLU_LIMIT)
    act = (lin + 1.0) * (gate * jax.nn.sigmoid(SWIGLU_ALPHA * gate))
    out = lax.ragged_dot(act, w_down, group_sizes) + b_down[e_sorted]
    out_pairs = jnp.zeros_like(out).at[order].set(out).reshape(T, TOP_K, D)
    y = jnp.einsum("tkd,tk->td", out_pairs, gates.astype(out.dtype))
    return y.reshape(B, S, D)

def setup_inputs(seed: int = 0) -> dict:
    key = jax.random.key(seed)
    ks = jax.random.split(key, 20)
    f32 = jnp.float32
    L, D, E, F = DEPTH, D_MODEL, N_EXPERTS, D_FF

    def nrm(k, shape, scale):
        return jax.random.normal(k, shape, f32) * scale

    return {
        "x": nrm(ks[0], (BATCH, SEQ, D), 1.0),
        "g_mix": 1.0 + nrm(ks[1], (L, D), 0.02),
        "w_in": nrm(ks[2], (L, D, IN_PROJ_W), D ** -0.5),
        "w_alpha_up": nrm(ks[3], (L, GLA_RANK, QK_W), GLA_RANK ** -0.5),
        "b_alpha": nrm(ks[4], (L, QK_W), 0.1),
        "g_gla": 1.0 + nrm(ks[5], (L, GLA_HEADS, GLA_DV), 0.02),
        "w_conv": nrm(ks[6], (L, CONV_K, CONV_WIDTH), CONV_K ** -0.5),
        "w_branch_a": nrm(ks[7], (L, V_W, D), V_W ** -0.5),
        "w_branch_b": nrm(ks[8], (L, CONV_WIDTH, D), CONV_WIDTH ** -0.5),
        "w_out": nrm(ks[9], (L, D, D), D ** -0.5),
        "g_ffn": 1.0 + nrm(ks[10], (L, D), 0.02),
        "w_router": nrm(ks[11], (L, D, E), D ** -0.5),
        "b_router": nrm(ks[12], (L, E), 0.01),
        "w_gate_up": nrm(ks[13], (L, E, D, 2 * F), D ** -0.5),
        "b_gate_up": nrm(ks[14], (L, E, 2 * F), 0.02),
        "w_down": nrm(ks[15], (L, E, F, D), F ** -0.5),
        "b_down": nrm(ks[16], (L, E, D), 0.02),
        "g_final": 1.0 + nrm(ks[17], (D,), 0.02),
    }

def reference(x, g_mix, w_in, w_alpha_up, b_alpha, g_gla, w_conv, w_branch_a, w_branch_b, w_out,
              g_ffn, w_router, b_router, w_gate_up, b_gate_up, w_down, b_down, g_final):
    B, S, _ = x.shape
    for l in range(DEPTH):
        h = rms_norm(x, g_mix[l])
        z = jnp.matmul(h, w_in[l])
        q, k, v, r, a_lr, c_b, c_c, c_x, g_a, g_b = split_columns(z)
        log_a = jax.nn.log_sigmoid(jnp.matmul(a_lr, w_alpha_up[l]) + b_alpha[l]) / GLA_TAU
        o = gla_chunked(q.reshape(B, S, GLA_HEADS, GLA_DK),
                        k.reshape(B, S, GLA_HEADS, GLA_DK),
                        v.reshape(B, S, GLA_HEADS, GLA_DV),
                        log_a.reshape(B, S, GLA_HEADS, GLA_DK))
        o = rms_norm(o, g_gla[l]) * jax.nn.silu(r).reshape(B, S, GLA_HEADS, GLA_DV)
        y_a = jnp.matmul(o.reshape(B, S, V_W), w_branch_a[l])
        y_conv = causal_dwconv(c_c * c_x, w_conv[l])
        y_b = jnp.matmul(c_b * y_conv, w_branch_b[l])
        mixed = jax.nn.sigmoid(g_a) * y_a + jax.nn.sigmoid(g_b) * y_b
        x = x + jnp.matmul(mixed, w_out[l])
        h = rms_norm(x, g_ffn[l])
        x = x + moe_ffn(h, w_router[l], b_router[l], w_gate_up[l], b_gate_up[l], w_down[l], b_down[l])
    return rms_norm(x, g_final)


_drawn_inputs = setup_inputs


def setup_inputs(seed=0):
    import zlib

    import numpy as np

    out = dict(_drawn_inputs(seed))
    spreads = {}
    factors = {'b_gate_up': 5.851, 'b_down': 6.732, 'g_final': 2.873}
    for name, (base, spread) in spreads.items():
        noise = np.random.default_rng([zlib.crc32(name.encode()), seed]).standard_normal(out[name].shape)
        drawn = base * np.exp(spread * noise) if base else spread * noise
        out[name] = __import__('jax').numpy.asarray(drawn.astype(out[name].dtype))
    for name, factor in factors.items():
        out[name] = (out[name] * factor).astype(out[name].dtype)
    return out
```

```python
from contextlib import ExitStack

import numpy as np

import concourse.bass as bass
from concourse import mybir

F32 = mybir.dt.float32
F32R = mybir.dt.float32r
BF16 = mybir.dt.bfloat16
I32 = mybir.dt.int32
U32 = mybir.dt.uint32
ALU = mybir.AluOpType
ACT = mybir.ActivationFunctionType
AX = mybir.AxisListType

P = 128
D = 1024
S = 1024
KT = D // P
TT = S // P
HEADS = 4
DK = D // 2 // HEADS
DV = D // HEADS
RANK = 16
TAU = 16.0
CHUNK = 64
CONV_K = 3
E = 32
TOP_K = 4
F = 1024
LIMIT = 7.0
ALPHA = 1.702
EPS = 1e-6
QK_W = HEADS * DK
V_W = HEADS * DV

COL_Q = 0
COL_K = COL_Q + QK_W
COL_V = COL_K + QK_W
COL_R = COL_V + V_W
COL_A = COL_R + V_W
COL_CB = COL_A + RANK
COL_CC = COL_CB + D
COL_CX = COL_CC + D
COL_GA = COL_CX + D
COL_GB = COL_GA + D

NP = 256
PANELS = D // NP
BPP = NP // P
HALF = S // 2
RB = 4

SUPER = 2 * P
MAX_SUPERS = S * TOP_K // SUPER + E - 1
W = MAX_SUPERS + 2
XROWS = S + P
KP = KT // 2
NW = 512
MP = 3 * F // NW * 2
GU = 2 * F // NW * 2
AHEAD = 6
WS = 6
RS = 3
OPEN = 2
NPOS = -16384.0


def f32(ap):
    return ap.bitcast(F32)


def panel_view(w):
    return w.rearrange("(k p) n -> p k n", p=P)


def product(pe, out, left_hi, left_lo, right_hi, right_lo, first=True, last=True, kts=range(KT)):
    kts = list(kts)
    for k in kts:
        pe.matmul(out, left_hi(k), right_hi(k), start=first and k == kts[0], stop=False,
                  skip_group_check=True)
        pe.matmul(out, left_hi(k), right_lo(k), start=False, stop=False, skip_group_check=True)
        mm = pe.matmul(out, left_lo(k), right_hi(k), start=False, stop=last and k == kts[-1],
                       skip_group_check=True)
    return mm


class Ring:

    def __init__(self, nc, ctx, tag):
        def sb(name, dt):
            return ctx.enter_context(nc.sbuf_tensor(f"{tag}_{name}", [P, 2, KT, NP], dt))

        self.raw = sb("raw", F32)
        self.hi = sb("whi", F32R)
        self.lo = sb("wlo", F32R)
        self.loaded = [ctx.enter_context(nc.semaphore(f"{tag}_loaded{s}")) for s in range(2)]
        self.hi_ready = ctx.enter_context(nc.semaphore(f"{tag}_hi_ready"))
        self.lo_ready = ctx.enter_context(nc.semaphore(f"{tag}_lo_ready"))

    def load(self, sp, n, src):
        if n >= 2:
            sp.wait_ge(self.lo_ready, n - 1)
        sp.dma_start(self.raw[:, n % 2], src).then_inc(self.loaded[n % 2], 16)

    def split_hi(self, act, s, t):
        act.wait_ge(self.loaded[s], 16 * t + 16)
        act.copy(self.hi[:, s], self.raw[:, s]).then_inc(self.hi_ready, 1)

    def split_lo(self, dve, s, t):
        dve.wait_ge(self.hi_ready, 2 * t + s + 1)
        dve.tensor_tensor(self.lo[:, s], self.raw[:, s], f32(self.hi[:, s]),
                          ALU.subtract).then_inc(self.lo_ready, 1)

    def right(self, s):
        return (lambda k: self.hi[:, s, k, :]), (lambda k: self.lo[:, s, k, :])

    def left(self, s, b):
        c = slice(b * P, (b + 1) * P)
        return (lambda k: self.hi[:, s, k, c]), (lambda k: self.lo[:, s, k, c])


def token_panels(pe, ring, pairs, first_pair, x_hi, x_lo, banks, ready, free, first_result):
    with pe.Fori(0, pairs) as t:
        for s in range(2):
            pe.wait_ge(ring.lo_ready, 2 * t + 2 * first_pair + s + 1)
            for i in range(TT):
                r = s * TT + i
                pe.wait_ge(free, 2 * TT * t + first_result + r + 1)
                c = slice(i * P, (i + 1) * P)
                hi, lo = ring.right(s)
                mm = product(pe, banks[r % len(banks)][:, 0:NP], lambda k: x_hi[:, k, c],
                             lambda k: x_lo[:, k, c], hi, lo)
                mm.then_inc(ready, 1)


def channel_panels(pe, ring, pairs, first_pair, x_hi, x_lo, banks, ready, free, first_result):
    with pe.Fori(0, pairs) as t:
        for s in range(2):
            pe.wait_ge(ring.lo_ready, 2 * t + 2 * first_pair + s + 1)
            for b in range(BPP):
                for h in range(2):
                    r = 4 * s + 2 * b + h
                    pe.wait_ge(free, 8 * t + first_result + r + 1)
                    c = slice(h * HALF, (h + 1) * HALF)
                    hi, lo = ring.left(s, b)
                    mm = product(pe, banks[r % len(banks)][:, :], hi, lo, lambda k: x_hi[:, k, c],
                                 lambda k: x_lo[:, k, c])
                    mm.then_inc(ready, 1)


def constants(nc, sb, cst):
    with ExitStack() as ctx:
        made = ctx.enter_context(nc.semaphore("const_made"))
        iota_i = ctx.enter_context(nc.sbuf_tensor("iota_i", [P, SUPER], I32))
        part_i = ctx.enter_context(nc.sbuf_tensor("part_i", [P, 1], I32))
        block = ctx.enter_context(nc.Block())

        @block.gpsimd
        def _(pool):
            n = 0

            def step(ins):
                nonlocal n
                n += 1
                ins.then_inc(made, 1)
                pool.wait_ge(made, n)

            step(pool.memset(cst["ident"][:, :], 0.0))
            step(pool.affine_select(out=cst["ident"][:, :], in_=cst["ident"][:, :], pattern=[[-1, P]],
                                    compare_op=ALU.not_equal, fill=1.0, base=0, channel_multiplier=1))
            step(pool.memset(cst["mask"][:, :], 1.0))
            step(pool.affine_select(out=cst["mask"][:, :], in_=cst["mask"][:, :], pattern=[[1, P]],
                                    compare_op=ALU.is_ge, fill=0.0, base=0, channel_multiplier=-1))
            step(pool.memset(cst["mask"][0:CHUNK, CHUNK:P], 0.0))
            step(pool.tensor_scalar(cst["cumul"][:, :], cst["mask"][:, :], 1.0 / TAU, None, ALU.mult))
            step(pool.memset(cst["before"][:, :], 1.0))
            step(pool.affine_select(out=cst["before"][:, :], in_=cst["before"][:, :], pattern=[[1, P]],
                                    compare_op=ALU.is_gt, fill=0.0, base=0, channel_multiplier=-1))
            step(pool.memset(cst["ones16"][:, :], 1.0))
            step(pool.iota(iota_i[:, :], pattern=[[1, SUPER]], base=0, channel_multiplier=0))
            step(pool.tensor_copy(cst["iota"][:, :], iota_i[:, :]))
            step(pool.iota(part_i[:, :], pattern=[[1, 1]], base=0, channel_multiplier=1))
            step(pool.tensor_copy(cst["part"][:, :], part_i[:, :]))
            step(pool.tensor_scalar(cst["spare"][:, 0:1], cst["part"][:, :], float(S), None, ALU.add))
            step(pool.tensor_scalar(cst["spare"][:, 1:2], cst["spare"][:, 0:1], -1.0, None, ALU.mult))
            step(pool.memset(cst["eps"][:, :], EPS))
            for i in range(TT):
                step(pool.tensor_copy(cst["tokens"][:, i, 0:1], cst["part"][:, :]))
                step(pool.memset(cst["tokens"][:, i, 1:2], float(i * P)))
                step(pool.memset(cst["tokens"][:, i, 2:3], 1.0))


def norm_and_transpose(nc, x, g_mix, w_in, cst, h_hi, h_lo, alpha_lr):
    w_view = panel_view(w_in)
    with ExitStack() as ctx:
        def sb(name, shape, dt=F32):
            return ctx.enter_context(nc.sbuf_tensor(f"n_{name}", shape, dt))

        def sem(name):
            return ctx.enter_context(nc.semaphore(f"n_{name}"))

        xt = sb("xt", [P, 2, D])
        junk = sb("junk", [P, D])
        ht = sb("ht", [P, 2, D])
        g = sb("g", [P, D])
        stat = sb("stat", [P, 3, 2])
        a_raw = sb("a_raw", [P, KT, P])
        a_hi = sb("a_hi", [P, KT, P], F32R)
        a_lo = sb("a_lo", [P, KT, P], F32R)
        turned = [ctx.enter_context(nc.psum_tensor(f"n_turned{s}", [P, D], F32)) for s in range(2)]
        a_out = [ctx.enter_context(nc.psum_tensor(f"n_a_out{h}", [P, HALF], F32)) for h in range(2)]

        x_loaded = [sem(f"x_loaded{s}") for s in range(2)]
        g_loaded, a_loaded = sem("g_loaded"), sem("a_loaded")
        squared, rooted, inverted = sem("squared"), sem("rooted"), sem("inverted")
        normed, transposed = sem("normed"), sem("transposed")
        hi_done, lo_done = sem("hi_done"), sem("lo_done")
        a_hi_done, a_lo_done, a_done, a_copied = (sem("a_hi_done"), sem("a_lo_done"), sem("a_done"),
                                                  sem("a_copied"))
        block = ctx.enter_context(nc.Block())

        @block.sync
        def _(sp):
            for i in range(TT):
                if i >= 2:
                    sp.wait_ge(normed, i - 1)
                sp.dma_start(xt[:, i % 2], x[i * P:(i + 1) * P, :]).then_inc(x_loaded[i % 2], 16)
                if i == 0:
                    sp.dma_start(g[:, :], g_mix.partition_broadcast(P)).then_inc(g_loaded, 16)
                if i == 1:
                    sp.dma_start(a_raw[:, :, :], w_view[:, :, COL_A:COL_A + P]).then_inc(a_loaded, 16)

        @block.scalar
        def _(act):
            with act.Fori(0, TT // 2) as t:
                for s in range(2):
                    act.wait_ge(x_loaded[s], 16 * t + 16)
                    if s:
                        act.wait_ge(squared, 2 * t + 1)
                    else:
                        act.wait_ge(squared, 2 * t)
                    act.activation(junk[:, :], xt[:, s], ACT.Square,
                                   accum_out=stat[:, 0, s:s + 1]).then_inc(squared, 1)
                act.wait_ge(squared, 2 * t + 2)
                act.activation(stat[:, 1, :], stat[:, 0, :], ACT.Sqrt, bias=cst["eps"][:, :],
                               scale=1.0 / D).then_inc(rooted, 1)
                for s in range(2):
                    act.wait_ge(transposed, 2 * t + s + 1)
                    act.copy(h_hi[:, :, bass.ds(t * 2 * P + s * P, P)],
                             turned[s][:, :].rearrange("p (k c) -> p k c", k=KT)).then_inc(hi_done, 1)
            act.wait_ge(a_loaded, 16)
            act.copy(a_hi[:, :, :], a_raw[:, :, :]).then_inc(a_hi_done, 1)
            for h in range(2):
                act.wait_ge(a_done, h + 1)
                act.copy(alpha_lr[:, h * HALF:(h + 1) * HALF], a_out[h][0:RANK, :]).then_inc(a_copied, 1)

        @block.vector
        def _(dve):
            dve.wait_ge(g_loaded, 16)
            with dve.Fori(0, TT // 2) as t:
                dve.wait_ge(rooted, t + 1)
                dve.reciprocal(stat[:, 2, :], stat[:, 1, :]).then_inc(inverted, 1)
                dve.wait_ge(inverted, t + 1)
                for s in range(2):
                    dve.scalar_tensor_tensor(out=ht[:, s], in0=xt[:, s], scalar=stat[:, 2, s:s + 1],
                                             in1=g[:, :], op0=ALU.mult, op1=ALU.mult).then_inc(normed, 1)
                for s in range(2):
                    dve.wait_ge(hi_done, 2 * t + s + 1)
                    c = bass.ds(t * 2 * P + s * P, P)
                    dve.tensor_tensor(h_lo[:, :, c], turned[s][:, :].rearrange("p (k c) -> p k c", k=KT),
                                      f32(h_hi[:, :, c]), ALU.subtract).then_inc(lo_done, 1)
            dve.wait_ge(a_hi_done, 1)
            dve.tensor_tensor(a_lo[:, :, :], a_raw[:, :, :], f32(a_hi[:, :, :]),
                              ALU.subtract).then_inc(a_lo_done, 1)

        @block.tensor
        def _(pe):
            with pe.Fori(0, TT // 2) as t:
                for s in range(2):
                    pe.wait_ge(normed, 2 * t + s + 1)
                    for k in range(KT):
                        tr = pe.transpose(turned[s][:, k * P:(k + 1) * P], ht[:, s, k * P:(k + 1) * P],
                                          cst["ident"][:, :])
                    tr.then_inc(transposed, 1)
            pe.wait_ge(lo_done, TT)
            pe.wait_ge(a_lo_done, 1)
            for h in range(2):
                c = slice(h * HALF, (h + 1) * HALF)
                mm = product(pe, a_out[h][:, :], lambda k: a_hi[:, k, :], lambda k: a_lo[:, k, :],
                             lambda k: h_hi[:, k, c], lambda k: h_lo[:, k, c])
                mm.then_inc(a_done, 1)


def project_qkv(nc, w_in, w_alpha_up, b_alpha, cst, h_hi, h_lo, alpha_lr, v, q, k, decay):
    w_view = panel_view(w_in)
    with ExitStack() as ctx:
        def sb(name, shape, dt=F32):
            return ctx.enter_context(nc.sbuf_tensor(f"q_{name}", shape, dt))

        def sem(name):
            return ctx.enter_context(nc.semaphore(f"q_{name}"))

        ring = Ring(nc, ctx, "q_ring")
        w_up = sb("w_up", [RANK, QK_W])
        b_up = sb("b_up", [P, QK_W])
        log_a = decay
        mag = sb("mag", [P, QK_W])
        soft = sb("soft", [P, QK_W])
        banks = [ctx.enter_context(nc.psum_tensor(f"q_bank{b}", [P, 512], F32)) for b in range(RB)]
        side = [ctx.enter_context(nc.psum_tensor(f"q_side{b}", [P, 512], F32)) for b in range(RB)]

        def heads(t):
            return t[:, :].rearrange("p (h n) -> p h n", h=HEADS)

        up_loaded = sem("up_loaded")
        ready, free = sem("ready"), sem("free")
        up_done, up_read = sem("up_done"), sem("up_read")
        mag_done, exp_done, soft_done, log_done = (sem("mag_done"), sem("exp_done"), sem("soft_done"),
                                                   sem("log_done"))
        sum_done, sum_read = sem("sum_done"), sem("sum_read")
        block = ctx.enter_context(nc.Block())

        @block.sync
        def _(sp):
            sp.dma_start(w_up[:, :], w_alpha_up).then_inc(up_loaded, 16)
            sp.dma_start(b_up[:, :], b_alpha.partition_broadcast(P)).then_inc(up_loaded, 16)
            cols = [COL_V + NP * n for n in range(PANELS)] + [COL_Q + NP * n for n in range(PANELS)]
            for n, c in enumerate(cols):
                ring.load(sp, n, w_view[:, :, c:c + NP])

        @block.scalar
        def _(act):
            act.sem_inc(free, RB)
            for s in range(2):
                ring.split_hi(act, s, 0)
            for i in range(TT):
                act.wait_ge(mag_done, i + 1)
                act.activation(soft[:, :], mag[:, :], ACT.Exp, scale=-1.0).then_inc(exp_done, 1)
                act.wait_ge(exp_done, i + 1)
                act.activation(soft[:, :], soft[:, :], ACT.Ln, bias=1.0).then_inc(soft_done, 1)
            with act.Fori(0, 2) as t:
                for s in range(2):
                    for i in range(TT):
                        r = s * TT + i
                        act.wait_ge(ready, 2 * TT * t + r + 1)
                        act.copy(v[:, i, bass.ds(t * 2 * NP + s * NP, NP)],
                                 banks[r % len(banks)][:, 0:NP]).then_inc(free, 1)
                    ring.split_hi(act, s, t + 1)
            for t in range(2):
                dst = q if t == 0 else k
                for s in range(2):
                    for b in range(BPP):
                        for h in range(2):
                            r = 4 * s + 2 * b + h
                            act.wait_ge(ready, 4 * TT + 8 * t + r + 1)
                            act.copy(dst[:, 2 * s + b, h * HALF:(h + 1) * HALF],
                                     banks[r % len(banks)][:, :]).then_inc(free, 1)
                    if t == 0:
                        ring.split_hi(act, s, 3)

        @block.vector
        def _(dve):
            for s in range(2):
                ring.split_lo(dve, s, 0)
            dve.wait_ge(up_loaded, 32)
            for i in range(TT):
                dve.wait_ge(up_done, i + 1)
                log_i = log_a[:, :, i * P:(i + 1) * P]
                dve.tensor_tensor(log_i, heads(side[i % RB]), heads(b_up), ALU.add).then_inc(up_read, 1)
                dve.wait_ge(up_read, i + 1)
                if i:
                    dve.wait_ge(exp_done, i)
                dve.scalar_tensor_tensor(out=heads(mag), in0=log_i, scalar=-1.0, in1=log_i,
                                         op0=ALU.mult, op1=ALU.max).then_inc(mag_done, 1)
                dve.wait_ge(soft_done, i + 1)
                dve.scalar_tensor_tensor(out=log_i, in0=log_i, scalar=0.0, in1=heads(soft),
                                         op0=ALU.min, op1=ALU.subtract).then_inc(log_done, 1)
            for t in range(1, 3):
                for s in range(2):
                    ring.split_lo(dve, s, t)
            for head in range(HEADS):
                for h in range(2):
                    n = 2 * head + h
                    dve.wait_ge(sum_done, 2 * head + 2)
                    dve.tensor_copy(decay[:, head, h * HALF:(h + 1) * HALF],
                                    side[n % RB][:, :]).then_inc(sum_read, 1)
            for s in range(2):
                ring.split_lo(dve, s, 3)

        @block.tensor
        def _(pe):
            pe.wait_ge(up_loaded, 32)
            for i in range(TT):
                if i >= RB:
                    pe.wait_ge(up_read, i - RB + 1)
                pe.matmul(side[i % RB][:, :], alpha_lr[:, i * P:(i + 1) * P], w_up[:, :], start=True,
                          stop=True).then_inc(up_done, 1)
            token_panels(pe, ring, 2, 0, h_hi, h_lo, banks, ready, free, 0)
            pe.wait_ge(log_done, TT)
            for head in range(HEADS):
                for h in range(2):
                    n = 2 * head + h
                    if n >= RB:
                        pe.wait_ge(sum_read, n - RB + 1)
                    for j in range(4):
                        mm = pe.matmul(side[n % RB][:, j * P:(j + 1) * P],
                                       log_a[:, head, h * HALF + j * P:h * HALF + (j + 1) * P],
                                       cst["cumul"][:, :],
                                       start=True, stop=True)
                    mm.then_inc(sum_done, 1)
            channel_panels(pe, ring, 2, 2, h_hi, h_lo, banks, ready, free, 4 * TT)


def linear_attention(nc, g_gla, cst, v, q, k, decay, inv_rms):
    with ExitStack() as ctx:
        def sb(name, shape, dt=F32):
            return ctx.enter_context(nc.sbuf_tensor(f"a_{name}", shape, dt))

        def sem(name):
            return ctx.enter_context(nc.semaphore(f"a_{name}"))

        def psum(name):
            return ctx.enter_context(nc.psum_tensor(f"a_{name}", [P, 512], F32))

        g = sb("g", [P, V_W])
        dtile = sb("dtile", [P, HEADS, P])
        qt, kt = sb("qt", [P, HEADS, P]), sb("kt", [P, HEADS, P])
        up = sb("up", [P, HEADS, P])
        down = sb("down", [P, HEADS, P])
        tail = sb("tail", [P, HEADS, P])
        keep = sb("keep", [P, HEADS, 2])
        q_dec, k_inv, k_tail = (sb("q_dec", [P, HEADS, P]), sb("k_inv", [P, HEADS, P]),
                                sb("k_tail", [P, HEADS, P]))
        scores = sb("scores", [P, HEADS, P])
        k_tok = sb("k_tok", [P, HEADS, P])
        vt = sb("vt", [P, V_W])
        state = sb("state", [P, 2, HEADS, DV])
        junk = sb("junk", [P, DV])
        squares = sb("squares", [P, TT, HEADS])
        p_scores, p_turn = psum("p_scores"), psum("p_turn")
        p_out = [psum(f"p_out{n}") for n in range(2)]
        p_up = [[psum(f"p_up{c}{n}") for n in range(2)] for c in range(2)]

        g_loaded, staged, decayed = sem("g_loaded"), sem("staged"), sem("decayed")
        q_ready, k_ready, tail_ready = sem("q_ready"), sem("k_ready"), sem("tail_ready")
        v_ready, scored, turned, masked, k_moved = (sem("v_ready"), sem("scored"), sem("turned"),
                                                    sem("masked"), sem("k_moved"))
        updated, stated = sem("updated"), sem("stated")
        out_done, squared, out_read = sem("out_done"), sem("squared"), sem("out_read")
        rooted, inverted, zeroed = sem("rooted"), sem("inverted"), sem("zeroed")
        block = ctx.enter_context(nc.Block())

        def head_cols(h):
            return slice((h % 2) * DV, (h % 2 + 1) * DV)

        @block.sync
        def _(sp):
            sp.dma_start(g[:, :], g_gla.partition_broadcast(P)).then_inc(g_loaded, 16)

        @block.gpsimd
        def _(pool):
            with pool.Fori(0, TT) as i:
                pool.wait_ge(out_done, HEADS * i)
                pool.tensor_copy(vt[:, :], v[:, bass.ds(i, 1), :].rearrange("p a n -> p (a n)")) \
                    .then_inc(v_ready, 1)

        @block.scalar
        def _(act):
            with act.Fori(0, TT) as i:
                act.wait_ge(staged, 3 * i + 1)
                act.wait_ge(tail_ready, i)
                act.activation(up[:, :, :], dtile[:, :, :], ACT.Exp).then_inc(decayed, 1)
                act.activation(down[:, :, :], dtile[:, :, :], ACT.Exp, scale=-1.0).then_inc(decayed, 1)
                for h in range(HEADS):
                    for c in range(2):
                        s = slice(c * CHUNK, (c + 1) * CHUNK)
                        act.activation(tail[:, h, s], dtile[:, h, s], ACT.Exp, scale=-1.0,
                                       bias=dtile[:, h, (c + 1) * CHUNK - 1:(c + 1) * CHUNK])
                act.wait_ge(stated, 2 * HEADS * i)
                act.activation(keep[:, :, :], dtile[:, :, CHUNK - 1::CHUNK], ACT.Exp).then_inc(decayed, 1)
                act.wait_ge(turned, i + 1)
                act.copy(k_tok[:, :, :].rearrange("p h n -> p (h n)"), p_turn[:, :]).then_inc(k_moved, 1)
                for h in range(HEADS):
                    act.wait_ge(out_done, HEADS * i + h + 1 if h % 2 else HEADS * i + h + 2)
                    act.wait_ge(squared, HEADS * i + h)
                    act.activation(junk[:, :], p_out[h // 2][:, head_cols(h)], ACT.Square,
                                   accum_out=squares[:, bass.ds(i, 1), h:h + 1].rearrange("p a n -> p (a n)")) \
                        .then_inc(squared, 1)
            act.wait_ge(squared, HEADS * TT)
            act.activation(squares[:, :, :], squares[:, :, :], ACT.Sqrt, bias=cst["eps"][:, :],
                           scale=1.0 / DV).then_inc(rooted, 1)

        @block.vector
        def _(dve):
            dve.memset(state[:, 0], 0.0).then_inc(zeroed, 1)
            dve.wait_ge(zeroed, 1)
            dve.wait_ge(g_loaded, 16)
            with dve.Fori(0, TT) as i:
                c = bass.ds(i * P, P)
                dve.tensor_copy(dtile[:, :, :], decay[:, :, c]).then_inc(staged, 1)
                dve.tensor_copy(qt[:, :, :], q[:, :, c]).then_inc(staged, 1)
                dve.tensor_copy(kt[:, :, :], k[:, :, c]).then_inc(staged, 1)
                dve.wait_ge(staged, 3 * i + 3)
                dve.wait_ge(decayed, 3 * i + 1)
                dve.scalar_tensor_tensor(out=q_dec[:, :, :], in0=qt[:, :, :], scalar=float(DK) ** -0.5,
                                         in1=up[:, :, :], op0=ALU.mult, op1=ALU.mult).then_inc(q_ready, 1)
                dve.wait_ge(decayed, 3 * i + 2)
                dve.tensor_tensor(k_inv[:, :, :], kt[:, :, :], down[:, :, :], ALU.mult).then_inc(k_ready, 1)
                dve.wait_ge(decayed, 3 * i + 3)
                dve.tensor_tensor(k_tail[:, :, :], kt[:, :, :], tail[:, :, :], ALU.mult) \
                    .then_inc(tail_ready, 1)
                dve.wait_ge(scored, i + 1)
                dve.tensor_tensor(scores[:, :, :], p_scores[:, :].rearrange("p (h n) -> p h n", h=HEADS),
                                  cst["mask"][:, :].unsqueeze(1).to_broadcast([P, HEADS, P]),
                                  ALU.mult).then_inc(masked, 1)
                dve.wait_ge(stated, 2 * HEADS * i)
                for ch in range(2):
                    for h in range(HEADS):
                        dve.wait_ge(updated, 2 * HEADS * i + HEADS * ch + (HEADS if h >= 2 else 2))
                        if ch == 1:
                            dve.wait_ge(stated, 2 * HEADS * i + h + 1)
                            dve.wait_ge(out_done, HEADS * i + h + 1)
                        dve.scalar_tensor_tensor(out=state[:, 1 - ch, h], in0=state[:, ch, h],
                                                 scalar=keep[:, h, ch:ch + 1],
                                                 in1=p_up[ch][h // 2][:, head_cols(h)],
                                                 op0=ALU.mult, op1=ALU.add).then_inc(stated, 1)
                for h in range(HEADS):
                    dve.wait_ge(squared, HEADS * i + (HEADS if h >= 2 else 2))
                    dve.tensor_tensor(v[:, bass.ds(i, 1), h * DV:(h + 1) * DV].rearrange("p a n -> p (a n)"),
                                      p_out[h // 2][:, head_cols(h)], g[:, h * DV:(h + 1) * DV],
                                      ALU.mult).then_inc(out_read, 1)
            dve.wait_ge(rooted, 1)
            dve.reciprocal(inv_rms[:, :, :], squares[:, :, :]).then_inc(inverted, 1)

        @block.tensor
        def _(pe):
            with pe.Fori(0, TT) as i:
                pe.wait_ge(q_ready, i + 1)
                pe.wait_ge(k_ready, i + 1)
                for h in range(HEADS):
                    mm = pe.matmul(p_scores[:, h * P:(h + 1) * P], k_inv[:, h], q_dec[:, h], start=True,
                                   stop=True)
                mm.then_inc(scored, 1)
                pe.wait_ge(tail_ready, i + 1)
                for h in range(HEADS):
                    mm = pe.transpose(p_turn[:, h * P:(h + 1) * P], k_tail[:, h], cst["ident"][:, :])
                mm.then_inc(turned, 1)
                pe.wait_ge(k_moved, i + 1)
                pe.wait_ge(v_ready, i + 1)
                for ch in range(2):
                    rows = slice(ch * CHUNK, (ch + 1) * CHUNK)
                    for h in range(HEADS):
                        pe.matmul(p_up[ch][h // 2][:, head_cols(h)], k_tok[rows, h], vt[rows, h * DV:(h + 1) * DV],
                                  start=True, stop=True).then_inc(updated, 1)
                pe.wait_ge(masked, i + 1)
                for h in range(HEADS):
                    out = p_out[h // 2][:, head_cols(h)]
                    vh = vt[:, h * DV:(h + 1) * DV]
                    pe.matmul(out, scores[:, h], vh, start=True, stop=False, skip_group_check=True)
                    pe.matmul(out[0:CHUNK], q_dec[:, h, 0:CHUNK], state[:, 0, h], start=False, stop=False,
                              skip_group_check=True)
                    pe.wait_ge(stated, 2 * HEADS * i + h + 1)
                    pe.matmul(out[CHUNK:P], q_dec[:, h, CHUNK:P], state[:, 1, h], start=False, stop=True,
                              skip_group_check=True).then_inc(out_done, 1)


def project_rest(nc, w_in, w_conv, h_hi, h_lo, o, inv_rms, y_conv, gates):
    w_view = panel_view(w_in)
    with ExitStack() as ctx:
        def sb(name, shape, dt=F32):
            return ctx.enter_context(nc.sbuf_tensor(f"r_{name}", shape, dt))

        def sem(name):
            return ctx.enter_context(nc.semaphore(f"r_{name}"))

        ring = Ring(nc, ctx, "r_ring")
        taps = sb("taps", [P, CONV_K, KT])
        sig = sb("sig", [P, 2, NP])
        silu = sb("silu", [P, 2, NP])
        cc = sb("cc", [P, BPP, S])
        u = sb("u", [P, BPP, CONV_K - 1 + S])
        y = sb("y", [P, BPP, S])
        gate = sb("gate", [P, 2, BPP, S])
        banks = [ctx.enter_context(nc.psum_tensor(f"r_bank{b}", [P, 512], F32)) for b in range(8)]

        taps_loaded, ready = sem("taps_loaded"), sem("ready")
        sig_done, silu_done, o_done = sem("sig_done"), sem("silu_done"), sem("o_done")
        cc_done, u_done, tap_done, y_done = sem("cc_done"), sem("u_done"), sem("tap_done"), sem("y_done")
        gate_done = sem("gate_done")
        y_stored, gate_stored = sem("y_stored"), [sem(f"gate_stored{s}") for s in range(2)]
        block = ctx.enter_context(nc.Block())

        R0 = 2 * 2 * TT
        C0 = 2 * 3 * PANELS * BPP

        @block.sync
        def _(sp):
            sp.dma_start(taps[:, :, :], w_conv.rearrange("i (b p) -> p i b", p=P),
                         allow_slow_non_contiguous=True).then_inc(taps_loaded, 16)
            cols = [COL_R + NP * n for n in range(PANELS)]
            for n in range(PANELS):
                cols += [COL_CC + NP * n, COL_CX + NP * n, COL_CB + NP * n]
            cols += [COL_GB + NP * n for n in range(PANELS)] + [COL_GA + NP * n for n in range(PANELS)]
            for n, c in enumerate(cols):
                ring.load(sp, n, w_view[:, :, c:c + NP])

        @block.gpsimd
        def _(pool):
            for n in range(PANELS):
                pool.wait_ge(y_done, 4 * (n + 1) + 4)
                pool.dma_start(y_conv[:, n * BPP:(n + 1) * BPP, :], y[:, :, :]).then_inc(y_stored, 16)
            for n in range(2 * PANELS):
                pool.wait_ge(gate_done, 4 * (n + 1) + 8)
                pool.dma_start(gates[:, n * BPP:(n + 1) * BPP, :], gate[:, n % 2]).then_inc(gate_stored[n % 2], 16)
            pool.wait_ge(y_stored, 16 * PANELS)
            for s in range(2):
                pool.wait_ge(gate_stored[s], 16 * PANELS)

        @block.scalar
        def _(act):
            act.sem_inc(gate_done, 8)
            for s in range(2):
                ring.split_hi(act, s, 0)
            with act.Fori(0, 2) as t:
                for s in range(2):
                    for i in range(TT):
                        r = s * TT + i
                        act.wait_ge(ready, 2 * TT * t + r + 1)
                        act.wait_ge(silu_done, 2 * TT * t + r - 1 + 8)
                        act.activation(sig[:, i % 2], banks[r % len(banks)][:, 0:NP], ACT.Sigmoid).then_inc(sig_done, 1)
                    ring.split_hi(act, s, t + 1)
            with act.Fori(0, PANELS // 2) as t:
                for n in range(6):
                    if n % 3 == 0:
                        for r in range(4):
                            act.wait_ge(ready, R0 + 24 * t + 4 * n + r + 1)
                            act.wait_ge(u_done, 8 * t + 4 * (n // 3) + 4)
                            act.copy(cc[:, r // 2, (r % 2) * HALF:(r % 2 + 1) * HALF],
                                     banks[4 * (n % 2) + r][:, :]) \
                                .then_inc(cc_done, 1)
                    act.wait_ge(ready, R0 + 24 * t + 4 * n + 4)
                    ring.split_hi(act, n % 2, 3 * t + n // 2 + 3)
            for n in range(2 * PANELS):
                for r in range(4):
                    act.wait_ge(ready, R0 + C0 + 4 * n + r + 1)
                    if n >= 2 and r == 0:
                        act.wait_ge(gate_stored[n % 2], 16 * (n // 2))
                    act.activation(gate[:, n % 2, r // 2, (r % 2) * HALF:(r % 2 + 1) * HALF],
                                   banks[4 * (n % 2) + r][:, :], ACT.Sigmoid).then_inc(gate_done, 1)
                if n + 2 < 2 * PANELS:
                    ring.split_hi(act, n % 2, (16 + n) // 2 + 1)

        @block.vector
        def _(dve):
            dve.memset(u[:, :, 0:CONV_K - 1], 0.0).then_inc(u_done, 4)
            dve.sem_inc(silu_done, 8)
            dve.sem_inc(y_done, 4)
            for s in range(2):
                ring.split_lo(dve, s, 0)
            with dve.Fori(0, 2) as t:
                for s in range(2):
                    for i in range(TT):
                        r = s * TT + i
                        dve.wait_ge(sig_done, 2 * TT * t + r + 1)
                        dve.wait_ge(o_done, 2 * TT * t + r)
                        dve.tensor_tensor(silu[:, i % 2], banks[r % len(banks)][:, 0:NP], sig[:, i % 2],
                                          ALU.mult).then_inc(silu_done, 1)
                        dve.wait_ge(silu_done, 2 * TT * t + r + 1 + 8)
                        o_i = o[:, i, bass.ds(t * 2 * NP + s * NP, NP)]
                        dve.scalar_tensor_tensor(out=o_i, in0=o_i, scalar=inv_rms[:, i, bass.ds(2 * t + s, 1)],
                                                 in1=silu[:, i % 2], op0=ALU.mult, op1=ALU.mult) \
                            .then_inc(o_done, 1)
                    ring.split_lo(dve, s, t + 1)
            dve.wait_ge(taps_loaded, 16)
            with dve.Fori(0, PANELS // 2) as t:
                for n in range(6):
                    if n % 3 == 1:
                        for r in range(4):
                            dve.wait_ge(cc_done, 8 * t + 4 * (n // 3) + r + 1)
                            dve.wait_ge(ready, R0 + 24 * t + 4 * n + r + 1)
                            c = slice((r % 2) * HALF, (r % 2 + 1) * HALF)
                            dve.tensor_tensor(u[:, r // 2, CONV_K - 1 + c.start:CONV_K - 1 + c.stop],
                                              banks[4 * (n % 2) + r][:, :], cc[:, r // 2, c], ALU.mult) \
                                .then_inc(u_done, 1)
                        dve.wait_ge(u_done, 8 * t + 4 * (n // 3) + 4 + 4)
                        dve.wait_ge(y_stored, 32 * t + 16 * (n // 3))
                        for i in range(CONV_K):
                            for b in range(BPP):
                                block_ = bass.ds(4 * t + 2 * (n // 3) + b, 1)
                                tap = taps[:, i, block_]
                                at = u[:, b, i:i + S]
                                if i == 0:
                                    dve.tensor_scalar(y[:, b], at, tap, None, ALU.mult).then_inc(tap_done, 1)
                                else:
                                    dve.wait_ge(tap_done, 12 * t + 6 * (n // 3) + 2 * (i - 1) + b + 1)
                                    dve.scalar_tensor_tensor(out=y[:, b], in0=at, scalar=tap, in1=y[:, b],
                                                             op0=ALU.mult, op1=ALU.add).then_inc(tap_done, 1)
                    if n % 3 == 2:
                        dve.wait_ge(tap_done, 12 * t + 6 * (n // 3) + 6)
                        for r in range(4):
                            dve.wait_ge(ready, R0 + 24 * t + 4 * n + r + 1)
                            c = slice((r % 2) * HALF, (r % 2 + 1) * HALF)
                            dve.tensor_tensor(y[:, r // 2, c], banks[4 * (n % 2) + r][:, :], y[:, r // 2, c],
                                              ALU.mult).then_inc(y_done, 1)
                    ring.split_lo(dve, n % 2, 3 * t + n // 2 + 3)
            for n in range(2 * PANELS):
                if n + 2 < 2 * PANELS:
                    ring.split_lo(dve, n % 2, (16 + n) // 2 + 1)

        @block.tensor
        def _(pe):
            token_panels(pe, ring, 2, 0, h_hi, h_lo, banks, ready, silu_done, 0)
            pe.wait_ge(silu_done, R0 + 8)
            with pe.Fori(0, PANELS // 2) as t:
                for n in range(6):
                    pe.wait_ge(ring.lo_ready, 6 * t + n + 5)
                    for b in range(BPP):
                        for h in range(2):
                            r = 2 * b + h
                            before = (u_done, y_done, cc_done)[n % 3]
                            pe.wait_ge(before, 8 * t + 4 * (n // 3) + r + 1)
                            c = slice(h * HALF, (h + 1) * HALF)
                            hi, lo = ring.left(n % 2, b)
                            mm = product(pe, banks[4 * (n % 2) + r][:, :], hi, lo,
                                         lambda k: h_hi[:, k, c], lambda k: h_lo[:, k, c])
                            mm.then_inc(ready, 1)
            pe.wait_ge(y_done, 4 * PANELS + 4)
            channel_panels(pe, ring, PANELS, 8, h_hi, h_lo, banks, ready, gate_done, 0)


def branch(nc, name, w, o, y_conv, gates, cst, mix):
    attention = o is not None
    with ExitStack() as ctx:
        def sb(n, shape, dt=F32):
            return ctx.enter_context(nc.sbuf_tensor(f"{name}_{n}", shape, dt))

        def sem(n):
            return ctx.enter_context(nc.semaphore(f"{name}_{n}"))

        ring = Ring(nc, ctx, f"{name}_ring")
        x_hi, x_lo = sb("x_hi", [P, KT, S], F32R), sb("x_lo", [P, KT, S], F32R)
        gate = sb("gate", [P, 2, BPP, S])
        banks = [ctx.enter_context(nc.psum_tensor(f"{name}_bank{b}", [P, 512], F32)) for b in range(RB)]
        if attention:
            turned = [ctx.enter_context(nc.psum_tensor(f"{name}_turned{s}", [P, D], F32)) for s in range(2)]
            part = sb("part", [P, 2, HALF])
        else:
            y = sb("y", [P, 2, S])
        y_loaded = [sem(f"y_loaded{s}") for s in range(2)]
        gate_loaded = [sem(f"gate_loaded{s}") for s in range(2)]
        transposed, hi_done, lo_done = sem("transposed"), sem("hi_done"), sem("lo_done")
        ready, taken, mixed = sem("ready"), sem("taken"), sem("mixed")
        block = ctx.enter_context(nc.Block())

        @block.sync
        def _(sp):
            for n in range(2):
                ring.load(sp, n, panel_view(w)[:, :, n * NP:(n + 1) * NP])
            if not attention:
                for j in range(KT):
                    if j >= 2:
                        sp.wait_ge(lo_done, j - 1)
                    sp.dma_start(y[:, j % 2], y_conv[:, j, :]).then_inc(y_loaded[j % 2], 16)
            for n in range(PANELS):
                if n == 2:
                    for m in range(2, PANELS):
                        ring.load(sp, m, panel_view(w)[:, :, m * NP:(m + 1) * NP])
                if n >= 2:
                    sp.wait_ge(taken, 4 * (n - 1) + RB)
                sp.dma_start(gate[:, n % 2], gates[:, n * BPP:(n + 1) * BPP, :]) \
                    .then_inc(gate_loaded[n % 2], 16)

        @block.scalar
        def _(act):
            for s in range(2):
                ring.split_hi(act, s, 0)
            for j in range(KT):
                if attention:
                    act.wait_ge(transposed, j + 1)
                    act.copy(x_hi[:, :, j * P:(j + 1) * P],
                             turned[j % 2][:, :].rearrange("p (k c) -> p k c", k=KT)).then_inc(hi_done, 1)
                else:
                    act.wait_ge(y_loaded[j % 2], 16 * (j // 2 + 1))
                    act.copy(x_hi[:, j], y[:, j % 2]).then_inc(hi_done, 1)
            for s in range(2):
                act.wait_ge(ready, 4 * s + 4)
                ring.split_hi(act, s, 1)

        @block.vector
        def _(dve):
            dve.sem_inc(taken, RB)
            for s in range(2):
                ring.split_lo(dve, s, 0)
            for j in range(KT):
                dve.wait_ge(hi_done, j + 1)
                if attention:
                    c = slice(j * P, (j + 1) * P)
                    dve.tensor_tensor(x_lo[:, :, c], turned[j % 2][:, :].rearrange("p (k c) -> p k c", k=KT),
                                      f32(x_hi[:, :, c]), ALU.subtract).then_inc(lo_done, 1)
                else:
                    dve.tensor_tensor(x_lo[:, j], y[:, j % 2], f32(x_hi[:, j]),
                                      ALU.subtract).then_inc(lo_done, 1)
            for n in range(PANELS):
                dve.wait_ge(gate_loaded[n % 2], 16 * (n // 2 + 1))
                for r in range(4):
                    k = 4 * n + r
                    dve.wait_ge(ready, k + 1)
                    c = slice((r % 2) * HALF, (r % 2 + 1) * HALF)
                    out = mix[:, n * BPP + r // 2, c]
                    if attention:
                        if k >= 2:
                            dve.wait_ge(mixed, k - 1)
                        dve.tensor_tensor(part[:, k % 2], banks[k % RB][:, :], gate[:, n % 2, r // 2, c],
                                          ALU.mult).then_inc(taken, 1)
                        dve.wait_ge(taken, k + 1 + RB)
                        dve.tensor_tensor(out, part[:, k % 2], out, ALU.add).then_inc(mixed, 1)
                    else:
                        dve.tensor_tensor(out, banks[k % RB][:, :], gate[:, n % 2, r // 2, c],
                                          ALU.mult).then_inc(taken, 1)
                if n < 2:
                    ring.split_lo(dve, n, 1)

        @block.tensor
        def _(pe):
            if attention:
                for i in range(TT):
                    if i >= 2:
                        pe.wait_ge(lo_done, i - 1)
                    for k in range(KT):
                        tr = pe.transpose(turned[i % 2][:, k * P:(k + 1) * P], o[:, i, k * P:(k + 1) * P],
                                          cst["ident"][:, :])
                    tr.then_inc(transposed, 1)
            pe.wait_ge(lo_done, KT)
            channel_panels(pe, ring, 2, 0, x_hi, x_lo, banks, ready, taken, 0)


def project_out(nc, w_out, x, mix, x2):
    with ExitStack() as ctx:
        def sem(n):
            return ctx.enter_context(nc.semaphore(f"o_{n}"))

        ring = Ring(nc, ctx, "o_ring")
        m_hi = ctx.enter_context(nc.sbuf_tensor("o_m_hi", [P, KT, S], F32R))
        m_lo = ctx.enter_context(nc.sbuf_tensor("o_m_lo", [P, KT, S], F32R))
        banks = [ctx.enter_context(nc.psum_tensor(f"o_bank{b}", [P, 512], F32)) for b in range(RB)]
        x_loaded, hi_done, lo_done = sem("x_loaded"), sem("hi_done"), sem("lo_done")
        ready, added = sem("ready"), sem("added")
        block = ctx.enter_context(nc.Block())

        @block.sync
        def _(sp):
            for n in range(PANELS):
                ring.load(sp, n, panel_view(w_out)[:, :, n * NP:(n + 1) * NP])
                if n == 1:
                    sp.dma_start(x2[:, :, :], x.rearrange("(i p) n -> p i n", p=P)).then_inc(x_loaded, 16)

        @block.scalar
        def _(act):
            for s in range(2):
                ring.split_hi(act, s, 0)
            for j in range(KT):
                act.copy(m_hi[:, j], mix[:, j]).then_inc(hi_done, 1)
            for s in range(2):
                act.wait_ge(ready, TT * (s + 1))
                ring.split_hi(act, s, 1)

        @block.vector
        def _(dve):
            dve.sem_inc(added, RB)
            for s in range(2):
                ring.split_lo(dve, s, 0)
            for j in range(KT):
                dve.wait_ge(hi_done, j + 1)
                dve.tensor_tensor(m_lo[:, j], mix[:, j], f32(m_hi[:, j]), ALU.subtract).then_inc(lo_done, 1)
            dve.wait_ge(x_loaded, 16)
            with dve.Fori(0, 2) as t:
                for s in range(2):
                    for i in range(TT):
                        r = s * TT + i
                        dve.wait_ge(ready, 2 * TT * t + r + 1)
                        out = x2[:, i, bass.ds(t * 2 * NP + s * NP, NP)]
                        dve.tensor_tensor(out, banks[r % RB][:, 0:NP], out, ALU.add).then_inc(added, 1)
                    if s == 0:
                        with dve.If(t < 1):
                            ring.split_lo(dve, 0, 1)
                    else:
                        with dve.If(t < 1):
                            ring.split_lo(dve, 1, 1)

        @block.tensor
        def _(pe):
            pe.wait_ge(lo_done, KT)
            token_panels(pe, ring, 2, 0, m_hi, m_lo, banks, ready, added, 0)


def route(nc, x2, g_ffn, w_router, b_router, h_rows, y_rows, cst, rank, gate3, table, row0):
    with ExitStack() as ctx:
        def sb(n, shape, dt=F32):
            return ctx.enter_context(nc.sbuf_tensor(f"g_{n}", shape, dt))

        def sem(n):
            return ctx.enter_context(nc.semaphore(f"g_{n}"))

        junk = sb("junk", [P, D])
        zero = sb("zero", [P, D])
        ht = sb("ht", [P, 2, D])
        hT = sb("hT", [P, 2, KT, P])
        g = sb("g", [P, D])
        wr = sb("wr", [P, KT, E])
        br = sb("br", [P, E])
        stat = sb("stat", [P, 3, 2])
        logits, top = sb("logits", [P, E]), sb("top", [P, 8])
        index, index_f = sb("index", [P, 8], U32), sb("index_f", [P, TOP_K])
        low, expo, total, inv = (sb("low", [P, 1]), sb("expo", [P, TOP_K]), sb("total", [P, 1]),
                                 sb("inv", [P, 1]))
        gates = sb("gates", [P, TOP_K])
        hot = sb("hot", [P, TOP_K, E])
        chosen = sb("chosen", [P, TT, E], BF16)
        weight = sb("weight", [P, TT, E])
        count, supers = sb("count", [P, E]), sb("supers", [P, E])
        scan = sb("scan", [P, 2, W])
        rows = sb("rows", [P, 8, W])
        cube = sb("cube", [P, W, E])
        rest = sb("rest", [P, TT, E])
        turned = [ctx.enter_context(nc.psum_tensor(f"g_turned{s}", [P, D], F32)) for s in range(2)]
        p_logits = [ctx.enter_context(nc.psum_tensor(f"g_logits{s}", [P, 512], F32)) for s in range(2)]
        p_rank = ctx.enter_context(nc.psum_tensor("g_rank", [P, 512], F32))

        loaded, zeroed = sem("loaded"), sem("zeroed")
        squared, rooted, inverted, normed = sem("squared"), sem("rooted"), sem("inverted"), sem("normed")
        transposed, moved, logged = sem("transposed"), sem("moved"), sem("logged")
        chain, expd, ranked = sem("chain"), sem("expd"), sem("ranked")
        waits_met = sem("waits_met")
        stored, finished = [sem(f"stored{s}") for s in range(2)], sem("finished")
        block = ctx.enter_context(nc.Block())
        STEPS = 11

        @block.sync
        def _(sp):
            sp.dma_start(g[:, :], g_ffn.partition_broadcast(P)).then_inc(loaded, 16)
            sp.dma_start(br[:, :], b_router.partition_broadcast(P)).then_inc(loaded, 16)
            sp.dma_start(wr[:, :, :], w_router.rearrange("(k p) e -> p k e", p=P)).then_inc(loaded, 16)
            sp.wait_ge(zeroed, 1)
            sp.dma_start(h_rows[S:XROWS, :], zero[:, :]).then_inc(finished, 16)
            sp.dma_start(y_rows[S:XROWS, :], zero[:, :]).then_inc(finished, 16)
            sp.dma_start(y_rows[0:S, :].rearrange("(i p) n -> p i n", p=P), x2[:, :, :]).then_inc(finished, 16)
            for i in range(TT):
                sp.wait_ge(normed, i + 1)
                sp.dma_start(h_rows[i * P:(i + 1) * P, :], ht[:, i % 2]).then_inc(stored[i % 2], 16)
            sp.wait_ge(finished, 48)
            for s in range(2):
                sp.wait_ge(stored[s], 16 * TT // 2)

        @block.scalar
        def _(act):
            with act.Fori(0, TT // 2) as t:
                for s in range(2):
                    act.wait_ge(squared, 2 * t + s)
                    act.activation(junk[:, :], x2[:, bass.ds(2 * t + s, 1), :].rearrange("p a n -> p (a n)"),
                                   ACT.Square, accum_out=stat[:, 0, s:s + 1]).then_inc(squared, 1)
                act.wait_ge(squared, 2 * t + 2)
                act.activation(stat[:, 1, :], stat[:, 0, :], ACT.Sqrt, bias=cst["eps"][:, :],
                               scale=1.0 / D).then_inc(rooted, 1)
                for s in range(2):
                    act.wait_ge(transposed, 2 * t + s + 1)
                    act.copy(hT[:, s].rearrange("p k c -> p (k c)"), turned[s][:, :]).then_inc(moved, 1)
                for s in range(2):
                    act.wait_ge(chain, 2 * STEPS * t + STEPS * s + 5)
                    act.activation(expo[:, :], top[:, 0:TOP_K], ACT.Exp, bias=low[:, :],
                                   accum_out=total[:, :]).then_inc(expd, 1)

        @block.vector
        def _(dve):
            dve.memset(zero[:, :], 0.0).then_inc(zeroed, 1)
            dve.wait_ge(loaded, 48)
            with dve.Fori(0, TT // 2) as t:
                dve.wait_ge(rooted, t + 1)
                dve.reciprocal(stat[:, 2, :], stat[:, 1, :]).then_inc(inverted, 1)
                dve.wait_ge(inverted, t + 1)
                for s in range(2):
                    dve.wait_ge(stored[s], 16 * t)
                    dve.scalar_tensor_tensor(out=ht[:, s],
                                             in0=x2[:, bass.ds(2 * t + s, 1), :].rearrange("p a n -> p (a n)"),
                                             scalar=stat[:, 2, s:s + 1],
                                             in1=g[:, :], op0=ALU.mult, op1=ALU.mult).then_inc(normed, 1)
                for s in range(2):
                    n = STEPS * s

                    def step(ins):
                        nonlocal n
                        n += 1
                        ins.then_inc(chain, 1)
                        dve.wait_ge(chain, 2 * STEPS * t + n)
                        dve.sem_inc(waits_met, 1)

                    i = bass.ds(2 * t + s, 1)
                    dve.wait_ge(logged, 2 * t + s + 1)
                    step(dve.tensor_tensor(logits[:, :], p_logits[s][:, 0:E], br[:, :], ALU.add))
                    step(dve.max(top[:, :], logits[:, :]))
                    step(dve.max_index(index[:, :], top[:, :], logits[:, :]))
                    step(dve.tensor_copy(index_f[:, :], index[:, 0:TOP_K]))
                    step(dve.tensor_scalar(low[:, :], top[:, 0:1], -1.0, None, ALU.mult))
                    dve.wait_ge(expd, 2 * t + s + 1)
                    step(dve.reciprocal(inv[:, :], total[:, :]))
                    step(dve.tensor_scalar(gates[:, :], expo[:, :], inv[:, 0:1], None, ALU.mult))
                    step(dve.tensor_tensor(hot[:, :, :],
                                           cst["iota"][:, 0:E].unsqueeze(1).to_broadcast([P, TOP_K, E]),
                                           index_f[:, :].unsqueeze(2).to_broadcast([P, TOP_K, E]),
                                           ALU.is_equal))
                    with nc.allow_low_precision(reason="sums of one 1 and zeros"):
                        step(dve.tensor_reduce(chosen[:, i, :].rearrange("p a e -> p (a e)"),
                                               hot[:, :, :].rearrange("p k e -> p e k"), AX.X, ALU.add))
                    step(dve.tensor_tensor(hot[:, :, :], hot[:, :, :],
                                           gates[:, :].unsqueeze(2).to_broadcast([P, TOP_K, E]), ALU.mult))
                    step(dve.tensor_reduce(weight[:, i, :].rearrange("p a e -> p (a e)"),
                                           hot[:, :, :].rearrange("p k e -> p e k"), AX.X, ALU.add))
                    assert n == STEPS * (s + 1)

            done = STEPS * TT

            def step(ins):
                nonlocal done
                done += 1
                ins.then_inc(chain, 1)
                dve.wait_ge(chain, done)

            dve.wait_ge(ranked, 1)
            pos = p_rank[:, 0:TT * E].rearrange("p (i e) -> p i e", i=TT)
            step(dve.scalar_tensor_tensor(out=rest[:, :, :], in0=pos, scalar=-NPOS, in1=chosen[:, :, :],
                                          op0=ALU.add, op1=ALU.mult))
            step(dve.tensor_scalar(rank[:, :, :], rest[:, :, :], NPOS, None, ALU.add))
            step(dve.tensor_copy(gate3[:, :, :, 0], weight[:, :, :]))
            step(dve.tensor_tensor(rest[:, :, :], weight[:, :, :], gate3[:, :, :, 0], ALU.subtract))
            step(dve.tensor_copy(gate3[:, :, :, 1], rest[:, :, :]))
            step(dve.tensor_tensor(weight[:, :, :], rest[:, :, :], gate3[:, :, :, 1], ALU.subtract))
            step(dve.tensor_copy(gate3[:, :, :, 2], weight[:, :, :]))
            step(dve.tensor_copy(count[:, :], p_rank[:, TT * E:(TT + 1) * E]))
            step(dve.tensor_scalar(supers[:, :], count[:, :], 0.0, None, ALU.is_gt))
            for m in range(SUPER, S, SUPER):
                step(dve.scalar_tensor_tensor(out=supers[:, :], in0=count[:, :], scalar=float(m),
                                              in1=supers[:, :], op0=ALU.is_gt, op1=ALU.add))

            def running_sum(src, width):
                step(dve.tensor_copy(scan[:, 0, 0:width], src))
                a, sh = 0, 1
                while sh < width:
                    step(dve.tensor_copy(scan[:, 1 - a, 0:sh], scan[:, a, 0:sh]))
                    step(dve.tensor_tensor(scan[:, 1 - a, sh:width], scan[:, a, sh:width],
                                           scan[:, a, 0:width - sh], ALU.add))
                    a, sh = 1 - a, 2 * sh
                return scan[:, a, 0:width]

            upto = running_sum(supers[:, :], E)
            number = cst["iota"][:, 0:W]
            wide = [P, W, E]
            expert, start, held, part, live, second, seconds, spare = (rows[:, r] for r in range(8))
            step(dve.tensor_tensor(cube[:, :, :], upto.unsqueeze(1).to_broadcast(wide),
                                   number.unsqueeze(2).to_broadcast(wide), ALU.is_le))
            step(dve.tensor_reduce(expert, cube[:, :, :], AX.X, ALU.add))
            step(dve.tensor_scalar(expert, expert, float(E - 1), None, ALU.min))
            step(dve.tensor_tensor(cube[:, :, :], cube[:, :, :],
                                   supers[:, :].unsqueeze(1).to_broadcast(wide), ALU.mult))
            step(dve.tensor_reduce(start, cube[:, :, :], AX.X, ALU.add))
            step(dve.tensor_tensor(part, number, start, ALU.subtract))
            step(dve.tensor_scalar(row0[:, :], part, float(SUPER), None, ALU.mult))
            step(dve.tensor_tensor(cube[:, :, :], cst["iota"][:, 0:E].unsqueeze(1).to_broadcast(wide),
                                   expert.unsqueeze(2).to_broadcast(wide), ALU.is_equal))
            step(dve.tensor_tensor(cube[:, :, :], cube[:, :, :],
                                   count[:, :].unsqueeze(1).to_broadcast(wide), ALU.mult))
            step(dve.tensor_reduce(held, cube[:, :, :], AX.X, ALU.add))
            step(dve.tensor_tensor(held, held, row0[:, :], ALU.subtract))
            step(dve.tensor_scalar(live, number, upto[:, E - 1:E], None, ALU.is_lt))
            step(dve.scalar_tensor_tensor(out=second, in0=held, scalar=float(P), in1=live, op0=ALU.is_gt,
                                          op1=ALU.mult))
            step(dve.tensor_copy(table[:, 3, 0:1], upto[:, E - 1:E]))
            total_seconds = running_sum(second, W)
            step(dve.tensor_tensor(seconds, total_seconds, second, ALU.subtract))
            step(dve.tensor_copy(table[:, 0], expert))
            step(dve.tensor_copy(table[:, 1], second))
            step(dve.tensor_copy(table[:, 2], seconds))

        @block.tensor
        def _(pe):
            pe.wait_ge(loaded, 48)
            with pe.Fori(0, TT // 2) as t:
                for s in range(2):
                    pe.wait_ge(normed, 2 * t + s + 1)
                    for k in range(KT):
                        tr = pe.transpose(turned[s][:, k * P:(k + 1) * P], ht[:, s, k * P:(k + 1) * P],
                                          cst["ident"][:, :])
                    tr.then_inc(transposed, 1)
                for s in range(2):
                    pe.wait_ge(moved, 2 * t + s + 1)
                    for k in range(KT):
                        mm = pe.matmul(p_logits[s][:, 0:E], hT[:, s, k], wr[:, k], start=(k == 0),
                                       stop=(k == KT - 1))
                    mm.then_inc(logged, 1)
            pe.wait_ge(chain, STEPS * TT)
            for i in range(TT + 1):
                out = p_rank[:, i * E:(i + 1) * E]
                for j in range(i):
                    mm = pe.matmul(out, cst["ones16"][:, :], chosen[:, j], start=(j == 0),
                                   stop=(j == TT - 1))
                if i < TT:
                    mm = pe.matmul(out, cst["before"][:, :], chosen[:, i], start=(i == 0), stop=True)
            mm.then_inc(ranked, 1)


def experts(nc, w_gate_up, b_gate_up, w_down, b_down, h_rows, y_rows, cst, rank, gate3, table, row0):
    gu_view = w_gate_up.rearrange("e (k p) n -> e p k n", p=P)
    dn_view = w_down.rearrange("e (k p) n -> e p k n", p=P)
    with ExitStack() as ctx:
        def sb(n, shape, dt=F32):
            return ctx.enter_context(nc.sbuf_tensor(f"m_{n}", shape, dt))

        signals = []

        def sem(n):
            signals.append(ctx.enter_context(nc.semaphore(f"m_{n}")))
            return signals[-1]

        def two(n):
            return [sem(f"{n}{x}") for x in range(2)]

        def psum(n):
            return ctx.enter_context(nc.psum_tensor(f"m_{n}", [P, 512], F32))

        raw = sb("raw", [P, RS, KP, NW])
        w_hi, w_lo = sb("w_hi", [P, WS, KP, NW], F32R), sb("w_lo", [P, WS, KP, NW], F32R)
        xg = sb("xg", [P, 2, D])
        x_hi, x_lo = sb("x_hi", [P, 2, KT, P], F32R), sb("x_lo", [P, 2, KT, P], F32R)
        a_tok = sb("a_tok", [P, 2, NW])
        a_hi, a_lo = sb("a_hi", [P, 2, KT, P], F32R), sb("a_lo", [P, 2, KT, P], F32R)
        y_out = sb("y_out", [P, 2, D])
        b_raw, b_split = sb("b_raw", [P, 2 * F]), sb("b_split", [P, 2 * F], F32R)
        pick = sb("pick", [P, 2, P], F32R)
        gate_t, sig_t = sb("gate_t", [P, 2, NW]), sb("sig_t", [P, 2, NW])
        place = sb("place", [P, TT])
        hits = sb("hits", [P, TT, SUPER], BF16)
        found = sb("found", [P, 2, 6])
        looked = sb("looked", [P, 2, 3])
        slot_next, slot_now = sb("slot_next", [P, 2], I32), sb("slot_now", [P, 2], I32)
        weight_next, weight_now = sb("weight_next", [P, 2]), sb("weight_now", [P, 2])
        pg = [[psum(f"pg{x}{b}") for b in range(2)] for x in range(2)]
        turn = [psum(f"turn{x}") for x in range(2)]
        p_found = psum("found_p")

        raw_loaded = [sem(f"raw_loaded{s}") for s in range(RS)]
        whi, wlo = sem("whi"), sem("wlo")
        bg_loaded, bg_hi, bg_lo = sem("bg_loaded"), sem("bg_hi"), sem("bg_lo")
        bd_loaded, bd_hi, bd_lo = sem("bd_loaded"), sem("bd_hi"), sem("bd_lo")
        prod = two("prod")
        clipped, taken, lin1 = two("clipped"), two("taken"), two("lin1")
        sig, activated = two("sig"), two("activated")
        turned, ahi, alo = two("turned"), two("ahi"), two("alo")
        x_turned, xhi, xlo = two("x_turned"), two("xhi"), two("xlo")
        y_done, scattered = two("y_done"), two("scattered")
        gathered, added = ([ctx.enter_context(nc.semaphore(f"m_{n}{x}")) for x in range(2)]
                           for n in ("gathered", "added"))
        placed, hit, counted = sem("placed"), sem("hit"), sem("counted")
        look, look_step, current = sem("look"), sem("look_step"), sem("current")
        waits_met = sem("waits_met")
        LOOKS = 5
        bias_cleared, split_cleared = sem("bias_cleared"), sem("split_cleared")
        for signal in signals:
            nc.gpsimd.sem_inc(signal, OPEN)
        nc.all_engine_barrier()
        block = ctx.enter_context(nc.Block())

        def load_value(eng, row, at, high):
            return eng.value_load(table[0:1, row, bass.ds(at, 1)], min_val=0, max_val=high)

        def per_tile(eng, t, nb, hb, body):
            body(0, t)
            with eng.If(hb > 0):
                body(1, nb)

        def seen(eng, sems, each, t, nb, hb, k):
            eng.wait_ge(sems[0], OPEN + each * t + k)
            eng.wait_ge(sems[1], OPEN + each * nb + k * hb)

        @block.sync
        def _(sp):
            supers = load_value(sp, 3, 0, MAX_SUPERS)

            def panel(m, e, g):
                if not (isinstance(g, int) and g + m < RS):
                    sp.wait_ge(wlo, OPEN + g + m - RS + 1)
                if m < GU:
                    c, k = (m // 2 % 2) * F + (m // 4) * NW, (m % 2) * KP
                    src = gu_view[bass.ds(e, 1), :, k:k + KP, c:c + NW]
                else:
                    c, k = (m % 2) * NW, ((m - GU) // 2) * KP
                    src = dn_view[bass.ds(e, 1), :, k:k + KP, c:c + NW]
                sp.dma_start(raw[:, m % RS], src.rearrange("a p k n -> p (a k) n")) \
                    .then_inc(raw_loaded[m % RS], 16)

            def gate_bias(e):
                for half in range(2):
                    for row in (32 * half, 64 + 32 * half):
                        sp.dma_start(b_raw[row:row + 1, 0:F], b_gate_up[bass.ds(e, 1), half * F:(half + 1) * F]) \
                            .then_inc(bg_loaded, 16)

            e = load_value(sp, 0, 0, E - 1)
            sp.wait_ge(bias_cleared, OPEN + 1)
            gate_bias(e)
            for m in range(AHEAD):
                panel(m, e, 0)
            with sp.Fori(0, supers) as t:
                e = load_value(sp, 0, t, E - 1)
                sp.wait_ge(bd_lo, OPEN + t)
                for row in (0, 64):
                    sp.dma_start(b_raw[row:row + 1, F:2 * F], b_down[bass.ds(e, 1), :]).then_inc(bd_loaded, 16)
                for m in range(AHEAD, MP):
                    panel(m, e, MP * t)
                e = load_value(sp, 0, t + 1, E - 1)
                sp.wait_ge(bg_lo, OPEN + t + 1)
                gate_bias(e)
                for m in range(AHEAD):
                    panel(m, e, MP * t + MP)

        @block.gpsimd
        def _(pool):
            pool.memset(b_raw[:, :], 0.0).then_inc(bias_cleared, 1)
            supers = load_value(pool, 3, 0, MAX_SUPERS)

            def lookup(t, n):
                e = load_value(pool, 0, t, E - 1)
                pool.wait_ge(counted, OPEN + n)
                pool.tensor_tensor(place[:, :], rank[:, :, bass.ds(e, 1)].rearrange("p i a -> p (i a)"),
                                   row0[:, bass.ds(t, 1)].to_broadcast([P, TT]), ALU.subtract) \
                    .then_inc(placed, 1)
                pool.wait_ge(placed, OPEN + n + 1)
                pool.sem_inc(waits_met, 1)
                for i in range(TT):
                    last = pool.tensor_scalar(hits[:, i], cst["iota"][:, :], place[:, i:i + 1], None,
                                              ALU.is_equal)
                last.then_inc(hit, 1)

            def gather(n):
                pool.wait_ge(look, OPEN + n + 1)
                pool.sem_inc(waits_met, 1)
                for x in range(2):
                    pool.indirect_dma_start(out=xg[:, x, :], out_offset=None, in_=h_rows[:, :],
                                            in_offset=bass.IndirectOffsetOnAxis(ap=slot_next[:, x:x + 1], axis=0)) \
                        .then_inc(gathered[x], 16)

            lookup(0, 0)
            gather(0)
            lookup(1, 1)
            with pool.Fori(0, supers) as t:
                hb = load_value(pool, 1, t, 1)
                nb = load_value(pool, 2, t, MAX_SUPERS)
                pool.wait_ge(x_turned[0], OPEN + t + 1)
                pool.wait_ge(x_turned[1], OPEN + nb + hb)
                gather(t + 1)
                lookup(t + 2, t + 2)

                def scatter(x, n):
                    pool.wait_ge(y_done[x], OPEN + 2 * n + 2)
                    pool.wait_ge(current, OPEN + t + 1)
                    pool.sem_inc(waits_met, 1)
                    pool.indirect_dma_start(out=y_rows[:, :],
                                            out_offset=bass.IndirectOffsetOnAxis(ap=slot_now[:, x:x + 1], axis=0),
                                            in_=y_out[:, x, :], in_offset=None, compute_op=ALU.add) \
                        .then_inc(added[x], 16)
                    pool.wait_ge(added[x], 16 * n + 16)
                    pool.sem_inc(scattered[x], 1)

                per_tile(pool, t, nb, hb, scatter)

        @block.scalar
        def _(act):
            supers = load_value(act, 3, 0, MAX_SUPERS)

            def split(m, t):
                act.wait_ge(raw_loaded[m % RS], OPEN + 16 * (MP // RS) * t + 16 * (m // RS) + 16)
                act.copy(w_hi[:, m % WS], raw[:, m % RS]).then_inc(whi, 1)

            def gate_bias(n):
                act.wait_ge(bg_loaded, OPEN + 64 * n + 64)
                act.copy(b_split[:, 0:F], b_raw[:, 0:F]).then_inc(bg_hi, 1)

            def x_split(x, n):
                act.wait_ge(x_turned[x], OPEN + n + 1)
                act.copy(x_hi[:, x, 0:4].rearrange("p k c -> p (k c)"), turn[0][:, :])
                act.copy(x_hi[:, x, 4:8].rearrange("p k c -> p (k c)"), turn[1][:, :]).then_inc(xhi[x], 1)

            act.wait_ge(bias_cleared, OPEN + 1)
            act.wait_ge(split_cleared, OPEN + 1)
            gate_bias(0)
            for m in range(AHEAD):
                split(m, 0)
            x_split(0, 0)
            with act.If(load_value(act, 1, 0, 1) > 0):
                x_split(1, 0)
            with act.Fori(0, supers) as t:
                hb = load_value(act, 1, t, 1)
                nb = load_value(act, 2, t, MAX_SUPERS)
                hb_next = load_value(act, 1, t + 1, 1)

                def sigmoid(j):
                    def body(x, n):
                        act.wait_ge(clipped[x], OPEN + 2 * n + j + 1)
                        act.activation(sig_t[:, x], gate_t[:, x], ACT.Sigmoid, scale=ALPHA).then_inc(sig[x], 1)
                    per_tile(act, t, nb, hb, body)

                def a_split(j):
                    def body(x, n):
                        act.wait_ge(turned[x], OPEN + 2 * n + j + 1)
                        act.copy(a_hi[:, x, KP * j:KP * (j + 1)].rearrange("p k c -> p (k c)"), turn[x][:, :]) \
                            .then_inc(ahi[x], 1)
                    per_tile(act, t, nb, hb, body)

                def store_y(b):
                    def body(x, n):
                        act.wait_ge(prod[x], OPEN + MP * n + MP - 1 + b)
                        act.wait_ge(current, OPEN + t + 1)
                        act.activation(y_out[:, x, b * 512:(b + 1) * 512], pg[x][b][:, :], ACT.Copy,
                                       scale=weight_now[:, x:x + 1]).then_inc(y_done[x], 1)
                    per_tile(act, t, nb, hb, body)

                for m in range(MP):
                    seen(act, prod, MP, t, nb, hb, m + 1)
                    if m in (2, 6):
                        sigmoid(m // 4)
                    if m in (5, 9):
                        a_split(m // 8)
                    if m == 7:
                        x_split(0, t + 1)
                    if m >= 10:
                        store_y(m - 10)
                    split((m + AHEAD) % MP, t + (m + AHEAD) // MP)
                    if m == 3:
                        act.wait_ge(bd_loaded, OPEN + 32 * t + 32)
                        act.copy(b_split[:, F:2 * F], b_raw[:, F:2 * F]).then_inc(bd_hi, 1)
                    if m == 8:
                        gate_bias(t + 1)
                with act.If(hb_next > 0):
                    x_split(1, nb + hb)

        @block.vector
        def _(dve):
            dve.memset(f32(b_split[:, :]), 0.0)
            dve.memset(f32(pick[:, :, :]), 0.0).then_inc(split_cleared, 1)
            supers = load_value(dve, 3, 0, MAX_SUPERS)
            dve.wait_ge(bias_cleared, OPEN + 1)
            dve.wait_ge(split_cleared, OPEN + 1)
            for x in range(2):
                for row in (32 * x, 64 + 32 * x):
                    dve.memset(f32(pick[row:row + 1, x, :]), 1.0)

            def split(m, g):
                dve.wait_ge(whi, OPEN + g + m + 1)
                dve.tensor_tensor(w_lo[:, m % WS], raw[:, m % RS], f32(w_hi[:, m % WS]),
                                  ALU.subtract).then_inc(wlo, 1)

            def bias(cols, hi, lo, n):
                dve.wait_ge(hi, OPEN + n + 1)
                dve.tensor_tensor(b_split[64:97, cols], b_raw[64:97, cols], f32(b_split[64:97, cols]),
                                  ALU.subtract).then_inc(lo, 1)

            def x_split(x, n):
                dve.wait_ge(xhi[x], OPEN + n + 1)
                dve.tensor_tensor(x_lo[:, x, 0:4].rearrange("p k c -> p (k c)"), turn[0][:, :],
                                  f32(x_hi[:, x, 0:4].rearrange("p k c -> p (k c)")), ALU.subtract)
                dve.tensor_tensor(x_lo[:, x, 4:8].rearrange("p k c -> p (k c)"), turn[1][:, :],
                                  f32(x_hi[:, x, 4:8].rearrange("p k c -> p (k c)")),
                                  ALU.subtract).then_inc(xlo[x], 1)

            def read_slots(n):
                dve.wait_ge(counted, OPEN + n + 1)
                k = LOOKS * n

                def step(ins, last=False):
                    nonlocal k
                    k = k + 1
                    if last:
                        ins.then_inc(look, 1)
                    else:
                        ins.then_inc(look_step, 1)
                        dve.wait_ge(look_step, OPEN + k)

                step(dve.tensor_copy(found[:, :, :], p_found[:, 0:12].rearrange("p (x c) -> p x c", x=2)))
                step(dve.tensor_tensor(looked[:, :, 0], found[:, :, 0], found[:, :, 1], ALU.add))
                step(dve.scalar_tensor_tensor(out=looked[:, :, 1], in0=found[:, :, 2],
                                              scalar=cst["spare"][:, 1:2], in1=looked[:, :, 0],
                                              op0=ALU.mult, op1=ALU.add))
                step(dve.tensor_tensor(looked[:, :, 2], found[:, :, 3], found[:, :, 4], ALU.add))
                step(dve.tensor_tensor(weight_next[:, :], looked[:, :, 2], found[:, :, 5], ALU.add))
                step(dve.tensor_scalar(slot_next[:, :], looked[:, :, 1], cst["spare"][:, 0:1], None, ALU.add),
                     last=True)

            bias(slice(0, F), bg_hi, bg_lo, 0)
            for m in range(AHEAD):
                split(m, 0)
            read_slots(0)
            x_split(0, 0)
            with dve.If(load_value(dve, 1, 0, 1) > 0):
                x_split(1, 0)
            with dve.Fori(0, supers) as t:
                hb = load_value(dve, 1, t, 1)
                nb = load_value(dve, 2, t, MAX_SUPERS)
                hb_next = load_value(dve, 1, t + 1, 1)

                def clip_gate(j):
                    def body(x, n):
                        dve.wait_ge(prod[x], OPEN + MP * n + 4 * j + 2)
                        dve.wait_ge(activated[x], OPEN + 2 * n + j)
                        dve.tensor_scalar(gate_t[:, x], pg[x][0][:, :], LIMIT, None, ALU.min) \
                            .then_inc(clipped[x], 1)
                    per_tile(dve, t, nb, hb, body)

                def activate(j):
                    def body(x, n):
                        dve.wait_ge(prod[x], OPEN + MP * n + 4 * j + 4)
                        dve.wait_ge(turned[x], OPEN + 2 * n + j)
                        dve.tensor_scalar(a_tok[:, x], pg[x][1][:, :], LIMIT, -LIMIT, ALU.min, ALU.max) \
                            .then_inc(taken[x], 1)
                        dve.wait_ge(taken[x], OPEN + 2 * n + j + 1)
                        dve.scalar_tensor_tensor(out=a_tok[:, x], in0=a_tok[:, x], scalar=1.0,
                                                 in1=gate_t[:, x], op0=ALU.add, op1=ALU.mult) \
                            .then_inc(lin1[x], 1)
                        dve.wait_ge(lin1[x], OPEN + 2 * n + j + 1)
                        dve.wait_ge(sig[x], OPEN + 2 * n + j + 1)
                        dve.tensor_tensor(a_tok[:, x], a_tok[:, x], sig_t[:, x], ALU.mult) \
                            .then_inc(activated[x], 1)
                    per_tile(dve, t, nb, hb, body)

                def a_split(j):
                    def body(x, n):
                        dve.wait_ge(ahi[x], OPEN + 2 * n + j + 1)
                        k = slice(KP * j, KP * (j + 1))
                        dve.tensor_tensor(a_lo[:, x, k].rearrange("p k c -> p (k c)"), turn[x][:, :],
                                          f32(a_hi[:, x, k].rearrange("p k c -> p (k c)")), ALU.subtract) \
                            .then_inc(alo[x], 1)
                    per_tile(dve, t, nb, hb, body)

                for m in range(MP):
                    if m in (1, 5):
                        clip_gate(m // 4)
                    if m in (3, 7):
                        activate(m // 4)
                    if m == 3:
                        dve.wait_ge(y_done[0], OPEN + 2 * t)
                        dve.wait_ge(y_done[1], OPEN + 2 * nb)
                        dve.wait_ge(scattered[0], OPEN + t)
                        dve.wait_ge(scattered[1], OPEN + nb)
                        dve.tensor_copy(weight_now[:, :], weight_next[:, :])
                        dve.tensor_copy(slot_now[:, :], slot_next[:, :]).then_inc(current, 1)
                        dve.wait_ge(gathered[0], 16 * t + 16)
                        dve.wait_ge(gathered[1], 16 * t + 16)
                        read_slots(t + 1)
                    if m in (5, 9):
                        a_split(m // 8)
                    if m == 8:
                        x_split(0, t + 1)
                    split((m + AHEAD) % MP, MP * (t + (m + AHEAD) // MP))
                    if m == 4:
                        bias(slice(F, 2 * F), bd_hi, bd_lo, t)
                    if m == 9:
                        bias(slice(0, F), bg_hi, bg_lo, t + 1)
                with dve.If(hb_next > 0):
                    x_split(1, nb + hb)

        @block.tensor
        def _(pe):
            supers = load_value(pe, 3, 0, MAX_SUPERS)

            def find(n, e):
                pe.wait_ge(hit, OPEN + n + 1)
                pe.wait_ge(look, OPEN + n)
                for x in range(2):
                    for src, c in ((lambda i: cst["tokens"][:, i, :], 0),
                                   (lambda i: gate3[:, i, bass.ds(e, 1), :].rearrange("p a c -> p (a c)"), 3)):
                        for i in range(TT):
                            mm = pe.matmul(p_found[:, 6 * x + c:6 * x + c + 3],
                                           hits[:, i, x * P:(x + 1) * P], src(i), start=(i == 0),
                                           stop=(i == TT - 1))
                mm.then_inc(counted, 1)

            def x_turn(x, n):
                for k in range(KT):
                    tr = pe.transpose(turn[k // 4][:, (k % 4) * P:(k % 4 + 1) * P], xg[:, x, k * P:(k + 1) * P],
                                      cst["ident"][:, :])
                tr.then_inc(x_turned[x], 1)

            find(0, load_value(pe, 0, 0, E - 1))
            pe.wait_ge(gathered[0], 16)
            x_turn(0, 0)
            with pe.If(load_value(pe, 1, 0, 1) > 0):
                pe.wait_ge(gathered[1], 16)
                pe.wait_ge(xlo[0], OPEN + 1)
                x_turn(1, 0)
            with pe.Fori(0, supers) as t:
                hb = load_value(pe, 1, t, 1)
                nb = load_value(pe, 2, t, MAX_SUPERS)
                hb_next = load_value(pe, 1, t + 1, 1)
                e_next = load_value(pe, 0, t + 1, E - 1)

                def panel(m):
                    down, bank = m >= GU, (m % 2 if m >= GU else m // 2 % 2)
                    kh = (m - GU) // 2 if down else m % 2

                    def body(x, n):
                        out = pg[x][bank][:, :]
                        if m == 0:
                            pe.wait_ge(xlo[x], OPEN + n + 1)
                        if m in (0, 2):
                            pe.wait_ge(y_done[x], OPEN + 2 * n - 1 + bank)
                        elif kh == 0:
                            pe.wait_ge(taken[x] if bank else clipped[x], OPEN + 2 * n + m // 4)
                        if down:
                            pe.wait_ge(alo[x], OPEN + 2 * n + kh + 1)
                        if kh == 0:
                            c = F + bank * NW if down else m // 4 * NW
                            pe.matmul(out, pick[:, 0 if down else bank, :], b_split[:, c:c + NW], start=True,
                                      stop=False, skip_group_check=True)
                        lh, ll = (a_hi, a_lo) if down else (x_hi, x_lo)
                        product(pe, out, lambda k: lh[:, x, KP * kh + k], lambda k: ll[:, x, KP * kh + k],
                                lambda k: w_hi[:, m % WS, k], lambda k: w_lo[:, m % WS, k],
                                first=False, last=(kh == 1), kts=range(KP)).then_inc(prod[x], 1)

                    pe.wait_ge(wlo, OPEN + MP * t + m + 1)
                    if m == 0:
                        pe.wait_ge(bg_lo, OPEN + t + 1)
                    if m == GU:
                        pe.wait_ge(bd_lo, OPEN + t + 1)
                    per_tile(pe, t, nb, hb, body)

                def a_turn(j):
                    def body(x, n):
                        pe.wait_ge(activated[x], OPEN + 2 * n + j + 1)
                        pe.wait_ge(alo[x], OPEN + 2 * n + j)
                        for b in range(KP):
                            tr = pe.transpose(turn[x][:, b * P:(b + 1) * P], a_tok[:, x, b * P:(b + 1) * P],
                                              cst["ident"][:, :])
                        tr.then_inc(turned[x], 1)
                    per_tile(pe, t, nb, hb, body)

                for m in range(MP):
                    panel(m)
                    if m == 1:
                        find(t + 1, e_next)
                    if m == 5:
                        a_turn(0)
                    if m == 7:
                        pe.wait_ge(gathered[0], 16 * t + 32)
                        seen(pe, alo, 2, t, nb, hb, 1)
                        x_turn(0, t + 1)
                    if m == 9:
                        pe.wait_ge(xlo[0], OPEN + t + 2)
                        a_turn(1)
                with pe.If(hb_next > 0):
                    pe.wait_ge(gathered[1], 16 * t + 32)
                    seen(pe, alo, 2, t, nb, hb, 2)
                    x_turn(1, nb + hb)


def finish(nc, y_rows, g_final, out, cst):
    with ExitStack() as ctx:
        def sb(n, shape, dt=F32):
            return ctx.enter_context(nc.sbuf_tensor(f"f_{n}", shape, dt))

        def sem(n):
            return ctx.enter_context(nc.semaphore(f"f_{n}"))

        yt, junk, ot, g = sb("yt", [P, TT, D]), sb("junk", [P, 2, D]), sb("ot", [P, TT, D]), sb("g", [P, D])
        stat = sb("stat", [P, 3, TT])
        loaded, g_loaded = [sem(f"loaded{i}") for i in range(TT)], sem("g_loaded")
        squared, rooted, inverted, normed, stored = (sem("squared"), sem("rooted"), sem("inverted"),
                                                     sem("normed"), sem("stored"))
        block = ctx.enter_context(nc.Block())

        @block.sync
        def _(sp):
            for i in range(TT):
                sp.dma_start(yt[:, i], y_rows[i * P:(i + 1) * P, :]).then_inc(loaded[i], 16)
                if i == 0:
                    sp.dma_start(g[:, :], g_final.partition_broadcast(P)).then_inc(g_loaded, 16)
            for i in range(TT):
                sp.wait_ge(normed, i + 1)
                sp.dma_start(out[i * P:(i + 1) * P, :], ot[:, i]).then_inc(stored, 16)
            sp.wait_ge(stored, 16 * TT)

        @block.scalar
        def _(act):
            for i in range(TT):
                act.wait_ge(loaded[i], 16)
                if i >= 2:
                    act.wait_ge(squared, i - 1)
                act.activation(junk[:, i % 2], yt[:, i], ACT.Square,
                               accum_out=stat[:, 0, i:i + 1]).then_inc(squared, 1)
                act.wait_ge(squared, i + 1)
                act.activation(stat[:, 1, i:i + 1], stat[:, 0, i:i + 1], ACT.Sqrt, bias=cst["eps"][:, :],
                               scale=1.0 / D).then_inc(rooted, 1)

        @block.vector
        def _(dve):
            dve.wait_ge(g_loaded, 16)
            for i in range(TT):
                dve.wait_ge(rooted, i + 1)
                dve.reciprocal(stat[:, 2, i:i + 1], stat[:, 1, i:i + 1]).then_inc(inverted, 1)
                dve.wait_ge(inverted, i + 1)
                dve.scalar_tensor_tensor(out=ot[:, i], in0=yt[:, i], scalar=stat[:, 2, i:i + 1], in1=g[:, :],
                                         op0=ALU.mult, op1=ALU.mult).then_inc(normed, 1)


def clear_signals(nc):
    nc.all_engine_barrier()
    used = set(nc.released_uncleared_semaphores)
    for first in sorted(n for n in used if n - 1 not in used):
        stop = first
        while stop in used:
            stop += 1
        nc.gpsimd.sem_clear(range(first, stop))
    nc.all_engine_barrier()


def decoder_block(nc, x, g_mix, w_in, w_alpha_up, b_alpha, g_gla, w_conv, w_branch_a, w_branch_b, w_out,
                  g_ffn, w_router, b_router, w_gate_up, b_gate_up, w_down, b_down, g_final, out):
    y_conv = nc.dram_tensor("y_conv", (P, KT, S), F32, kind="Internal").ap()
    gates = nc.dram_tensor("gates", (P, 2 * KT, S), F32, kind="Internal").ap()
    h_rows = nc.dram_tensor("h_rows", (XROWS, D), F32, kind="Internal").ap()
    y_rows = nc.dram_tensor("y_rows", (XROWS, D), F32, kind="Internal").ap()

    with ExitStack() as whole:
        def sb(ctx, name, shape, dt=F32):
            return ctx.enter_context(nc.sbuf_tensor(name, shape, dt))

        cst = {"ident": sb(whole, "ident", [P, P]), "iota": sb(whole, "iota", [P, SUPER]),
               "tokens": sb(whole, "tokens", [P, TT, 3], BF16), "spare": sb(whole, "spare", [P, 2]),
               "eps": sb(whole, "eps", [P, 1]), "part": sb(whole, "part", [P, 1])}
        rank = sb(whole, "rank", [P, TT, E])
        gate3 = sb(whole, "gate3", [P, TT, E, 3], BF16)
        table = sb(whole, "table", [P, 4, W], I32)
        row0 = sb(whole, "row0", [P, W])

        with ExitStack() as mixer:
            cst["mask"] = sb(mixer, "mask", [P, P])
            cst["cumul"] = sb(mixer, "cumul", [P, P])
            cst["before"] = sb(mixer, "before", [P, P], BF16)
            cst["ones16"] = sb(mixer, "ones16", [P, P], BF16)
            constants(nc, sb, cst)
            with ExitStack() as upto_branches:
                v = sb(upto_branches, "v", [P, TT, V_W])
                with ExitStack() as projections:
                    h_hi = sb(projections, "h_hi", [P, KT, S], F32R)
                    h_lo = sb(projections, "h_lo", [P, KT, S], F32R)
                    inv_rms = sb(projections, "inv_rms", [P, TT, HEADS])
                    with ExitStack() as recurrence:
                        q, k = (sb(recurrence, "q", [P, HEADS, S]), sb(recurrence, "k", [P, HEADS, S]))
                        decay = sb(recurrence, "decay", [P, HEADS, S])
                        alpha_lr = k[0:RANK, 0]
                        norm_and_transpose(nc, x, g_mix, w_in, cst, h_hi, h_lo, alpha_lr)
                        project_qkv(nc, w_in, w_alpha_up, b_alpha, cst, h_hi, h_lo, alpha_lr, v, q, k, decay)
                        linear_attention(nc, g_gla, cst, v, q, k, decay, inv_rms)
                    project_rest(nc, w_in, w_conv, h_hi, h_lo, v, inv_rms, y_conv, gates)
                mix = sb(upto_branches, "mix", [P, KT, S])
                branch(nc, "b", w_branch_b, None, y_conv, gates[:, 0:KT, :], cst, mix)
                branch(nc, "a", w_branch_a, v, None, gates[:, KT:2 * KT, :], cst, mix)
                x2 = v
                project_out(nc, w_out, x, mix, x2)
                route(nc, x2, g_ffn, w_router, b_router, h_rows, y_rows, cst, rank, gate3, table, row0)
        clear_signals(nc)
        experts(nc, w_gate_up, b_gate_up, w_down, b_down, h_rows, y_rows, cst, rank, gate3, table, row0)
        finish(nc, y_rows, g_final, out, cst)


_INS = ["x", "g_mix", "w_in", "w_alpha_up", "b_alpha", "g_gla", "w_conv", "w_branch_a", "w_branch_b", "w_out",
        "g_ffn", "w_router", "b_router", "w_gate_up", "b_gate_up", "w_down", "b_down", "g_final"]


def kernel(**inputs):
    import concourse.bacc as bacc
    from concourse.bass_utils import run_bass_kernel_spmd

    nc = bacc.Bacc("TRN2", target_bir_lowering=False, num_devices=1)
    arrays, args = {}, []
    for name in _INS:
        a = np.ascontiguousarray(inputs[name])
        arrays[f"in_{name}"] = a
        t = nc.dram_tensor(f"in_{name}", a.shape, mybir.dt.from_np(a.dtype), kind="ExternalInput").ap()
        if name == "x":
            t = t.rearrange("b s d -> (b s) d")
        elif name == "g_gla":
            t = t.rearrange("l h v -> (l h v)")
        elif name == "g_final":
            pass
        elif len(a.shape) == 2:
            t = t.rearrange("l n -> (l n)")
        elif len(a.shape) == 3:
            t = t.rearrange("l a b -> (l a) b")
        else:
            t = t.rearrange("l e a b -> (l e) a b")
        args.append(t)
    out = nc.dram_tensor("out_0", (1, S, D), F32, kind="ExternalOutput").ap()
    decoder_block(nc, *args, out.rearrange("b s d -> (b s) d"))
    r = run_bass_kernel_spmd(nc, [arrays], core_ids=[0])
    return r.results[0]["out_0"]
```

```python
from contextlib import ExitStack

import numpy as np

import concourse.bass as bass
from concourse import mybir

F32 = mybir.dt.float32
F32R = mybir.dt.float32r
BF16 = mybir.dt.bfloat16
I32 = mybir.dt.int32
U32 = mybir.dt.uint32
ALU = mybir.AluOpType
ACT = mybir.ActivationFunctionType
AX = mybir.AxisListType

P = 128
D = 1024
S = 1024
KT = D // P
TT = S // P
HEADS = 4
DK = D // 2 // HEADS
DV = D // HEADS
RANK = 16
TAU = 16.0
CHUNK = 64
CONV_K = 3
E = 32
TOP_K = 4
F = 1024
LIMIT = 7.0
ALPHA = 1.702
EPS = 1e-6
QK_W = HEADS * DK
V_W = HEADS * DV

COL_Q = 0
COL_K = COL_Q + QK_W
COL_V = COL_K + QK_W
COL_R = COL_V + V_W
COL_A = COL_R + V_W
COL_CB = COL_A + RANK
COL_CC = COL_CB + D
COL_CX = COL_CC + D
COL_GA = COL_CX + D
COL_GB = COL_GA + D

NP = 256
PANELS = D // NP
BPP = NP // P
HALF = S // 2
RB = 4

SUPER = 2 * P
MAX_SUPERS = S * TOP_K // SUPER + E - 1
W = MAX_SUPERS + 2
XROWS = S + P
KP = KT // 2
NW = 512
MP = 3 * F // NW * 2
GU = 2 * F // NW * 2
AHEAD = 6
WS = 6
RS = 4
OPEN = 2
NPOS = -16384.0


def f32(ap):
    return ap.bitcast(F32)


def panel_view(w):
    return w.rearrange("(k p) n -> p k n", p=P)


def product(pe, out, left_hi, left_lo, right_hi, right_lo, first=True, last=True, kts=range(KT)):
    kts = list(kts)
    for k in kts:
        pe.matmul(out, left_hi(k), right_hi(k), start=first and k == kts[0], stop=False,
                  skip_group_check=True)
        pe.matmul(out, left_hi(k), right_lo(k), start=False, stop=False, skip_group_check=True)
        mm = pe.matmul(out, left_lo(k), right_hi(k), start=False, stop=last and k == kts[-1],
                       skip_group_check=True)
    return mm


class Ring:

    def __init__(self, nc, ctx, tag):
        def sb(name, dt):
            return ctx.enter_context(nc.sbuf_tensor(f"{tag}_{name}", [P, 2, KT, NP], dt))

        self.raw = sb("raw", F32)
        self.hi = sb("whi", F32R)
        self.lo = sb("wlo", F32R)
        self.loaded = [ctx.enter_context(nc.semaphore(f"{tag}_loaded{s}")) for s in range(2)]
        self.hi_ready = ctx.enter_context(nc.semaphore(f"{tag}_hi_ready"))
        self.lo_ready = ctx.enter_context(nc.semaphore(f"{tag}_lo_ready"))

    def load(self, sp, n, src):
        if n >= 2:
            sp.wait_ge(self.lo_ready, n - 1)
        sp.dma_start(self.raw[:, n % 2], src).then_inc(self.loaded[n % 2], 16)

    def split_hi(self, act, s, t):
        act.wait_ge(self.loaded[s], 16 * t + 16)
        act.copy(self.hi[:, s], self.raw[:, s]).then_inc(self.hi_ready, 1)

    def split_lo(self, dve, s, t):
        dve.wait_ge(self.hi_ready, 2 * t + s + 1)
        dve.tensor_tensor(self.lo[:, s], self.raw[:, s], f32(self.hi[:, s]),
                          ALU.subtract).then_inc(self.lo_ready, 1)

    def right(self, s):
        return (lambda k: self.hi[:, s, k, :]), (lambda k: self.lo[:, s, k, :])

    def left(self, s, b):
        c = slice(b * P, (b + 1) * P)
        return (lambda k: self.hi[:, s, k, c]), (lambda k: self.lo[:, s, k, c])


def by_contraction(pe, outs, operands, opened, kt_done, ready):
    for k in range(KT):
        pe.wait_ge(kt_done, k + 1)
        for r, (out, (left_hi, left_lo, right_hi, right_lo)) in enumerate(zip(outs, operands)):
            if k == 0:
                opened(r)
            mm = product(pe, out, left_hi, left_lo, right_hi, right_lo, first=(k == 0), last=(k == KT - 1),
                         kts=[k])
            if k == KT - 1:
                mm.then_inc(ready, 1)


def token_panels(pe, ring, pairs, first_pair, x_hi, x_lo, banks, ready, free, first_result, kt_done=None):
    with pe.Fori(0, pairs) as t:
        for s in range(2):
            pe.wait_ge(ring.lo_ready, 2 * t + 2 * first_pair + s + 1)
            first = 0
            if kt_done is not None and s == 0:
                first = RB
                hi, lo = ring.right(s)
                by_contraction(pe, [banks[i][:, 0:NP] for i in range(RB)],
                               [(lambda k, i=i: x_hi[:, k, i * P:(i + 1) * P],
                                 lambda k, i=i: x_lo[:, k, i * P:(i + 1) * P], hi, lo) for i in range(RB)],
                               lambda i: pe.wait_ge(free, 2 * TT * t + first_result + i + 1), kt_done, ready)
            for i in range(first, TT):
                r = s * TT + i
                pe.wait_ge(free, 2 * TT * t + first_result + r + 1)
                c = slice(i * P, (i + 1) * P)
                hi, lo = ring.right(s)
                mm = product(pe, banks[r % len(banks)][:, 0:NP], lambda k: x_hi[:, k, c],
                             lambda k: x_lo[:, k, c], hi, lo)
                mm.then_inc(ready, 1)


def channel_panels(pe, ring, pairs, first_pair, x_hi, x_lo, banks, ready, free, first_result, kt_done=None):
    with pe.Fori(0, pairs) as t:
        for s in range(2):
            pe.wait_ge(ring.lo_ready, 2 * t + 2 * first_pair + s + 1)
            if kt_done is not None and s == 0:
                by_contraction(pe, [banks[r][:, :] for r in range(RB)],
                               [(*ring.left(s, r // 2), lambda k, r=r: x_hi[:, k, r % 2 * HALF:(r % 2 + 1) * HALF],
                                 lambda k, r=r: x_lo[:, k, r % 2 * HALF:(r % 2 + 1) * HALF]) for r in range(RB)],
                               lambda r: pe.wait_ge(free, 8 * t + first_result + r + 1), kt_done, ready)
                continue
            for b in range(BPP):
                for h in range(2):
                    r = 4 * s + 2 * b + h
                    pe.wait_ge(free, 8 * t + first_result + r + 1)
                    c = slice(h * HALF, (h + 1) * HALF)
                    hi, lo = ring.left(s, b)
                    mm = product(pe, banks[r % len(banks)][:, :], hi, lo, lambda k: x_hi[:, k, c],
                                 lambda k: x_lo[:, k, c])
                    mm.then_inc(ready, 1)


def constants(nc, sb, cst):
    with ExitStack() as ctx:
        made = ctx.enter_context(nc.semaphore("const_made"))
        iota_i = ctx.enter_context(nc.sbuf_tensor("iota_i", [P, SUPER], I32))
        part_i = ctx.enter_context(nc.sbuf_tensor("part_i", [P, 1], I32))
        block = ctx.enter_context(nc.Block())

        @block.gpsimd
        def _(pool):
            n = 0

            def step(ins):
                nonlocal n
                n += 1
                ins.then_inc(made, 1)
                pool.wait_ge(made, n)

            step(pool.memset(cst["ident"][:, :], 0.0))
            step(pool.affine_select(out=cst["ident"][:, :], in_=cst["ident"][:, :], pattern=[[-1, P]],
                                    compare_op=ALU.not_equal, fill=1.0, base=0, channel_multiplier=1))
            step(pool.memset(cst["mask"][:, :], 1.0))
            step(pool.affine_select(out=cst["mask"][:, :], in_=cst["mask"][:, :], pattern=[[1, P]],
                                    compare_op=ALU.is_ge, fill=0.0, base=0, channel_multiplier=-1))
            step(pool.memset(cst["mask"][0:CHUNK, CHUNK:P], 0.0))
            step(pool.tensor_scalar(cst["cumul"][:, :], cst["mask"][:, :], 1.0 / TAU, None, ALU.mult))
            step(pool.memset(cst["before"][:, :], 1.0))
            step(pool.affine_select(out=cst["before"][:, :], in_=cst["before"][:, :], pattern=[[1, P]],
                                    compare_op=ALU.is_gt, fill=0.0, base=0, channel_multiplier=-1))
            step(pool.memset(cst["ones16"][:, :], 1.0))
            step(pool.iota(iota_i[:, :], pattern=[[1, SUPER]], base=0, channel_multiplier=0))
            step(pool.tensor_copy(cst["iota"][:, :], iota_i[:, :]))
            step(pool.iota(part_i[:, :], pattern=[[1, 1]], base=0, channel_multiplier=1))
            step(pool.tensor_copy(cst["part"][:, :], part_i[:, :]))
            step(pool.tensor_scalar(cst["spare"][:, 0:1], cst["part"][:, :], float(S), None, ALU.add))
            step(pool.tensor_scalar(cst["spare"][:, 1:2], cst["spare"][:, 0:1], -1.0, None, ALU.mult))
            step(pool.memset(cst["eps"][:, :], EPS))
            for i in range(TT):
                step(pool.tensor_copy(cst["tokens"][:, i, 0:1], cst["part"][:, :]))
                step(pool.memset(cst["tokens"][:, i, 1:2], float(i * P)))
                step(pool.memset(cst["tokens"][:, i, 2:3], 1.0))


def norm_and_transpose(nc, x, g_mix, w_in, cst, h_hi, h_lo, alpha_lr, xt):
    w_view = panel_view(w_in)
    with ExitStack() as ctx:
        def sb(name, shape, dt=F32):
            return ctx.enter_context(nc.sbuf_tensor(f"n_{name}", shape, dt))

        def sem(name):
            return ctx.enter_context(nc.semaphore(f"n_{name}"))

        junk = sb("junk", [P, D])
        ht = sb("ht", [P, 2, D])
        g = sb("g", [P, D])
        stat = sb("stat", [P, 3, TT])
        a_raw = sb("a_raw", [P, KT, P])
        a_hi = sb("a_hi", [P, KT, P], F32R)
        a_lo = sb("a_lo", [P, KT, P], F32R)
        turned = [ctx.enter_context(nc.psum_tensor(f"n_turned{s}", [P, D], F32)) for s in range(2)]
        a_out = [ctx.enter_context(nc.psum_tensor(f"n_a_out{h}", [P, HALF], F32)) for h in range(2)]

        x_loaded = [sem(f"x_loaded{i}") for i in range(TT)]
        g_loaded, a_loaded = sem("g_loaded"), sem("a_loaded")
        squared, rooted, inverted = sem("squared"), sem("rooted"), sem("inverted")
        normed, transposed = sem("normed"), sem("transposed")
        hi_done, lo_done = sem("hi_done"), sem("lo_done")
        a_hi_done, a_lo_done, a_done, a_copied = (sem("a_hi_done"), sem("a_lo_done"), sem("a_done"),
                                                  sem("a_copied"))
        block = ctx.enter_context(nc.Block())

        @block.sync
        def _(sp):
            for i in range(TT):
                sp.dma_start(xt[:, i], x[i * P:(i + 1) * P, :]).then_inc(x_loaded[i], 16)
                if i == 1:
                    sp.dma_start(g[:, :], g_mix.partition_broadcast(P)).then_inc(g_loaded, 16)
            sp.dma_start(a_raw[:, :, :], w_view[:, :, COL_A:COL_A + P]).then_inc(a_loaded, 16)

        @block.scalar
        def _(act):
            for half in range(2):
                for i in range(4 * half, 4 * half + 4):
                    act.wait_ge(x_loaded[i], 16)
                    if i:
                        act.wait_ge(squared, i)
                    act.activation(junk[:, :], xt[:, i], ACT.Square,
                                   accum_out=stat[:, 0, i:i + 1]).then_inc(squared, 1)
                c = slice(4 * half, 4 * half + 4)
                act.wait_ge(squared, 4 * half + 4)
                act.activation(stat[:, 1, c], stat[:, 0, c], ACT.Sqrt, bias=cst["eps"][:, :],
                               scale=1.0 / D).then_inc(rooted, 1)
            for i in range(TT):
                act.wait_ge(transposed, i + 1)
                act.copy(h_hi[:, :, i * P:(i + 1) * P],
                         turned[i % 2][:, :].rearrange("p (k c) -> p k c", k=KT)).then_inc(hi_done, 1)
            act.wait_ge(a_loaded, 16)
            act.copy(a_hi[:, :, :], a_raw[:, :, :]).then_inc(a_hi_done, 1)
            for h in range(2):
                act.wait_ge(a_done, h + 1)
                act.copy(alpha_lr[:, h * HALF:(h + 1) * HALF], a_out[h][0:RANK, :]).then_inc(a_copied, 1)

        @block.vector
        def _(dve):
            dve.wait_ge(g_loaded, 16)

            def norm(i):
                if i % 4 == 0:
                    c = slice(i, i + 4)
                    dve.wait_ge(rooted, i // 4 + 1)
                    dve.reciprocal(stat[:, 2, c], stat[:, 1, c]).then_inc(inverted, 1)
                    dve.wait_ge(inverted, i // 4 + 1)
                if i >= 2:
                    dve.wait_ge(transposed, i - 1)
                dve.scalar_tensor_tensor(out=ht[:, i % 2], in0=xt[:, i], scalar=stat[:, 2, i:i + 1],
                                         in1=g[:, :], op0=ALU.mult, op1=ALU.mult).then_inc(normed, 1)

            norm(0)
            norm(1)
            for i in range(TT):
                if i + 2 < TT:
                    norm(i + 2)
                dve.wait_ge(hi_done, i + 1)
                c = slice(i * P, (i + 1) * P)
                dve.tensor_tensor(h_lo[:, :, c], turned[i % 2][:, :].rearrange("p (k c) -> p k c", k=KT),
                                  f32(h_hi[:, :, c]), ALU.subtract).then_inc(lo_done, 1)
            dve.wait_ge(a_hi_done, 1)
            dve.tensor_tensor(a_lo[:, :, :], a_raw[:, :, :], f32(a_hi[:, :, :]),
                              ALU.subtract).then_inc(a_lo_done, 1)

        @block.tensor
        def _(pe):
            for i in range(TT):
                pe.wait_ge(normed, i + 1)
                if i >= 2:
                    pe.wait_ge(lo_done, i - 1)
                for k in range(KT):
                    tr = pe.transpose(turned[i % 2][:, k * P:(k + 1) * P], ht[:, i % 2, k * P:(k + 1) * P],
                                      cst["ident"][:, :])
                tr.then_inc(transposed, 1)
            pe.wait_ge(lo_done, TT)
            pe.wait_ge(a_lo_done, 1)
            for h in range(2):
                c = slice(h * HALF, (h + 1) * HALF)
                mm = product(pe, a_out[h][:, :], lambda k: a_hi[:, k, :], lambda k: a_lo[:, k, :],
                             lambda k: h_hi[:, k, c], lambda k: h_lo[:, k, c])
                mm.then_inc(a_done, 1)


def project_qkv(nc, w_in, w_alpha_up, b_alpha, cst, h_hi, h_lo, alpha_lr, v, q, k, decay):
    w_view = panel_view(w_in)
    with ExitStack() as ctx:
        def sb(name, shape, dt=F32):
            return ctx.enter_context(nc.sbuf_tensor(f"q_{name}", shape, dt))

        def sem(name):
            return ctx.enter_context(nc.semaphore(f"q_{name}"))

        ring = Ring(nc, ctx, "q_ring")
        w_up = sb("w_up", [RANK, QK_W])
        b_up = sb("b_up", [P, QK_W])
        log_a = decay
        mag = sb("mag", [P, QK_W])
        soft = sb("soft", [P, QK_W])
        banks = [ctx.enter_context(nc.psum_tensor(f"q_bank{b}", [P, 512], F32)) for b in range(RB)]
        side = [ctx.enter_context(nc.psum_tensor(f"q_side{b}", [P, 512], F32)) for b in range(RB)]

        def heads(t):
            return t[:, :].rearrange("p (h n) -> p h n", h=HEADS)

        up_loaded = sem("up_loaded")
        ready, free = sem("ready"), sem("free")
        up_done, up_read = sem("up_done"), sem("up_read")
        mag_done, exp_done, soft_done, log_done = (sem("mag_done"), sem("exp_done"), sem("soft_done"),
                                                   sem("log_done"))
        sum_done, sum_read = sem("sum_done"), sem("sum_read")
        block = ctx.enter_context(nc.Block())

        @block.sync
        def _(sp):
            sp.dma_start(w_up[:, :], w_alpha_up).then_inc(up_loaded, 16)
            sp.dma_start(b_up[:, :], b_alpha.partition_broadcast(P)).then_inc(up_loaded, 16)
            cols = [COL_V + NP * n for n in range(PANELS)] + [COL_Q + NP * n for n in range(PANELS)]
            for n, c in enumerate(cols):
                ring.load(sp, n, w_view[:, :, c:c + NP])

        @block.scalar
        def _(act):
            act.sem_inc(free, RB)
            for s in range(2):
                ring.split_hi(act, s, 0)
            for i in range(TT):
                act.wait_ge(mag_done, i + 1)
                act.activation(soft[:, :], mag[:, :], ACT.Exp, scale=-1.0).then_inc(exp_done, 1)
                act.wait_ge(exp_done, i + 1)
                act.activation(soft[:, :], soft[:, :], ACT.Ln, bias=1.0).then_inc(soft_done, 1)
            with act.Fori(0, 2) as t:
                for s in range(2):
                    for i in range(TT):
                        r = s * TT + i
                        act.wait_ge(ready, 2 * TT * t + r + 1)
                        act.copy(v[:, i, bass.ds(t * 2 * NP + s * NP, NP)],
                                 banks[r % len(banks)][:, 0:NP]).then_inc(free, 1)
                    ring.split_hi(act, s, t + 1)
            for t in range(2):
                dst = q if t == 0 else k
                for s in range(2):
                    for b in range(BPP):
                        for h in range(2):
                            r = 4 * s + 2 * b + h
                            act.wait_ge(ready, 4 * TT + 8 * t + r + 1)
                            act.copy(dst[:, 2 * s + b, h * HALF:(h + 1) * HALF],
                                     banks[r % len(banks)][:, :]).then_inc(free, 1)
                    if t == 0:
                        ring.split_hi(act, s, 3)

        @block.vector
        def _(dve):
            for s in range(2):
                ring.split_lo(dve, s, 0)
            dve.wait_ge(up_loaded, 32)
            for i in range(TT):
                dve.wait_ge(up_done, i + 1)
                log_i = log_a[:, :, i * P:(i + 1) * P]
                dve.tensor_tensor(log_i, heads(side[i % RB]), heads(b_up), ALU.add).then_inc(up_read, 1)
                dve.wait_ge(up_read, i + 1)
                if i:
                    dve.wait_ge(exp_done, i)
                dve.scalar_tensor_tensor(out=heads(mag), in0=log_i, scalar=-1.0, in1=log_i,
                                         op0=ALU.mult, op1=ALU.max).then_inc(mag_done, 1)
                dve.wait_ge(soft_done, i + 1)
                dve.scalar_tensor_tensor(out=log_i, in0=log_i, scalar=0.0, in1=heads(soft),
                                         op0=ALU.min, op1=ALU.subtract).then_inc(log_done, 1)
            for t in range(1, 3):
                for s in range(2):
                    ring.split_lo(dve, s, t)
            for head in range(HEADS):
                for h in range(2):
                    n = 2 * head + h
                    dve.wait_ge(sum_done, 2 * head + 2)
                    dve.tensor_copy(decay[:, head, h * HALF:(h + 1) * HALF],
                                    side[n % RB][:, :]).then_inc(sum_read, 1)
            for s in range(2):
                ring.split_lo(dve, s, 3)

        @block.tensor
        def _(pe):
            pe.wait_ge(up_loaded, 32)
            for i in range(TT):
                if i >= RB:
                    pe.wait_ge(up_read, i - RB + 1)
                pe.matmul(side[i % RB][:, :], alpha_lr[:, i * P:(i + 1) * P], w_up[:, :], start=True,
                          stop=True).then_inc(up_done, 1)
            token_panels(pe, ring, 2, 0, h_hi, h_lo, banks, ready, free, 0)
            pe.wait_ge(log_done, TT)
            for head in range(HEADS):
                for h in range(2):
                    n = 2 * head + h
                    if n >= RB:
                        pe.wait_ge(sum_read, n - RB + 1)
                    for j in range(4):
                        mm = pe.matmul(side[n % RB][:, j * P:(j + 1) * P],
                                       log_a[:, head, h * HALF + j * P:h * HALF + (j + 1) * P],
                                       cst["cumul"][:, :],
                                       start=True, stop=True)
                    mm.then_inc(sum_done, 1)
            channel_panels(pe, ring, 2, 2, h_hi, h_lo, banks, ready, free, 4 * TT)


def linear_attention(nc, g_gla, cst, v, q, k, decay, inv_rms):
    with ExitStack() as ctx:
        def sb(name, shape, dt=F32):
            return ctx.enter_context(nc.sbuf_tensor(f"a_{name}", shape, dt))

        def sem(name):
            return ctx.enter_context(nc.semaphore(f"a_{name}"))

        def psum(name):
            return ctx.enter_context(nc.psum_tensor(f"a_{name}", [P, 512], F32))

        g = sb("g", [P, V_W])
        dtile = sb("dtile", [P, HEADS, P])
        qt, kt = sb("qt", [P, HEADS, P]), sb("kt", [P, HEADS, P])
        up = sb("up", [P, HEADS, P])
        down = sb("down", [P, HEADS, P])
        tail = sb("tail", [P, HEADS, P])
        keep = sb("keep", [P, HEADS, 2])
        q_dec, k_inv, k_tail = (sb("q_dec", [P, HEADS, P]), sb("k_inv", [P, HEADS, P]),
                                sb("k_tail", [P, HEADS, P]))
        scores = sb("scores", [P, HEADS, P])
        k_tok = sb("k_tok", [P, HEADS, P])
        vt = sb("vt", [P, V_W])
        state = sb("state", [P, 2, HEADS, DV])
        junk = sb("junk", [P, DV])
        squares = sb("squares", [P, TT, HEADS])
        p_scores, p_turn = psum("p_scores"), psum("p_turn")
        p_out = [psum(f"p_out{n}") for n in range(2)]
        p_up = [[psum(f"p_up{c}{n}") for n in range(2)] for c in range(2)]

        g_loaded, staged, decayed = sem("g_loaded"), sem("staged"), sem("decayed")
        q_ready, k_ready, tail_ready = sem("q_ready"), sem("k_ready"), sem("tail_ready")
        v_ready, scored, turned, masked, k_moved = (sem("v_ready"), sem("scored"), sem("turned"),
                                                    sem("masked"), sem("k_moved"))
        updated, stated = sem("updated"), sem("stated")
        out_done, squared, out_read = sem("out_done"), sem("squared"), sem("out_read")
        rooted, inverted, zeroed = sem("rooted"), sem("inverted"), sem("zeroed")
        block = ctx.enter_context(nc.Block())

        def head_cols(h):
            return slice((h % 2) * DV, (h % 2 + 1) * DV)

        @block.sync
        def _(sp):
            sp.dma_start(g[:, :], g_gla.partition_broadcast(P)).then_inc(g_loaded, 16)

        @block.gpsimd
        def _(pool):
            with pool.Fori(0, TT) as i:
                pool.wait_ge(out_done, HEADS * i + 1)
                pool.tensor_copy(vt[:, :], v[:, bass.ds(i, 1), :].rearrange("p a n -> p (a n)")) \
                    .then_inc(v_ready, 1)

        @block.scalar
        def _(act):
            act.sem_inc(squared, 1)
            with act.Fori(0, TT) as i:
                act.wait_ge(tail_ready, i + 1)
                act.wait_ge(staged, 3 * i + 1)
                act.activation(up[:, :, :], dtile[:, :, :], ACT.Exp).then_inc(decayed, 1)
                act.activation(down[:, :, :], dtile[:, :, :], ACT.Exp, scale=-1.0).then_inc(decayed, 1)
                for h in range(HEADS):
                    for c in range(2):
                        s = slice(c * CHUNK, (c + 1) * CHUNK)
                        act.activation(tail[:, h, s], dtile[:, h, s], ACT.Exp, scale=-1.0,
                                       bias=dtile[:, h, (c + 1) * CHUNK - 1:(c + 1) * CHUNK])
                act.wait_ge(stated, 2 * HEADS * i + 1)
                act.activation(keep[:, :, :], dtile[:, :, CHUNK - 1::CHUNK], ACT.Exp).then_inc(decayed, 1)
                act.wait_ge(turned, i + 1)
                act.copy(k_tok[:, :, :].rearrange("p h n -> p (h n)"), p_turn[:, :]).then_inc(k_moved, 1)
                for h in range(HEADS):
                    act.wait_ge(out_done, HEADS * i + (h + 2 if h % 2 else h + 3))
                    act.wait_ge(squared, HEADS * i + (h + 1))
                    act.activation(junk[:, :], p_out[h // 2][:, head_cols(h)], ACT.Square,
                                   accum_out=squares[:, bass.ds(i, 1), h:h + 1].rearrange("p a n -> p (a n)")) \
                        .then_inc(squared, 1)
            act.wait_ge(squared, HEADS * TT + 1)
            act.activation(squares[:, :, :], squares[:, :, :], ACT.Sqrt, bias=cst["eps"][:, :],
                           scale=1.0 / DV).then_inc(rooted, 1)

        @block.vector
        def _(dve):
            dve.sem_inc(tail_ready, 1)
            dve.sem_inc(stated, 1)
            dve.memset(state[:, 0], 0.0).then_inc(zeroed, 1)
            dve.wait_ge(zeroed, 1)
            dve.wait_ge(g_loaded, 16)
            with dve.Fori(0, TT) as i:
                c = bass.ds(i * P, P)
                dve.tensor_copy(dtile[:, :, :], decay[:, :, c]).then_inc(staged, 1)
                dve.tensor_copy(qt[:, :, :], q[:, :, c]).then_inc(staged, 1)
                dve.tensor_copy(kt[:, :, :], k[:, :, c]).then_inc(staged, 1)
                dve.wait_ge(staged, 3 * i + 3)
                dve.wait_ge(decayed, 3 * i + 1)
                dve.scalar_tensor_tensor(out=q_dec[:, :, :], in0=qt[:, :, :], scalar=float(DK) ** -0.5,
                                         in1=up[:, :, :], op0=ALU.mult, op1=ALU.mult).then_inc(q_ready, 1)
                dve.wait_ge(decayed, 3 * i + 2)
                dve.tensor_tensor(k_inv[:, :, :], kt[:, :, :], down[:, :, :], ALU.mult).then_inc(k_ready, 1)
                dve.wait_ge(decayed, 3 * i + 3)
                dve.tensor_tensor(k_tail[:, :, :], kt[:, :, :], tail[:, :, :], ALU.mult) \
                    .then_inc(tail_ready, 1)
                dve.wait_ge(scored, i + 1)
                dve.tensor_tensor(scores[:, :, :], p_scores[:, :].rearrange("p (h n) -> p h n", h=HEADS),
                                  cst["mask"][:, :].unsqueeze(1).to_broadcast([P, HEADS, P]),
                                  ALU.mult).then_inc(masked, 1)
                dve.wait_ge(stated, 2 * HEADS * i + 1)
                for ch in range(2):
                    for h in range(HEADS):
                        dve.wait_ge(updated, 2 * HEADS * i + HEADS * ch + (HEADS if h >= 2 else 2))
                        if ch == 1:
                            dve.wait_ge(stated, 2 * HEADS * i + (h + 2))
                            dve.wait_ge(out_done, HEADS * i + (h + 2))
                        dve.scalar_tensor_tensor(out=state[:, 1 - ch, h], in0=state[:, ch, h],
                                                 scalar=keep[:, h, ch:ch + 1],
                                                 in1=p_up[ch][h // 2][:, head_cols(h)],
                                                 op0=ALU.mult, op1=ALU.add).then_inc(stated, 1)
                for h in range(HEADS):
                    dve.wait_ge(squared, HEADS * i + (HEADS + 1 if h >= 2 else 3))
                    dve.tensor_tensor(v[:, bass.ds(i, 1), h * DV:(h + 1) * DV].rearrange("p a n -> p (a n)"),
                                      p_out[h // 2][:, head_cols(h)], g[:, h * DV:(h + 1) * DV],
                                      ALU.mult).then_inc(out_read, 1)
            dve.wait_ge(rooted, 1)
            dve.reciprocal(inv_rms[:, :, :], squares[:, :, :]).then_inc(inverted, 1)

        @block.tensor
        def _(pe):
            pe.sem_inc(out_done, 1)
            with pe.Fori(0, TT) as i:
                pe.wait_ge(q_ready, i + 1)
                pe.wait_ge(k_ready, i + 1)
                for h in range(HEADS):
                    mm = pe.matmul(p_scores[:, h * P:(h + 1) * P], k_inv[:, h], q_dec[:, h], start=True,
                                   stop=True)
                mm.then_inc(scored, 1)
                pe.wait_ge(tail_ready, i + 2)
                for h in range(HEADS):
                    mm = pe.transpose(p_turn[:, h * P:(h + 1) * P], k_tail[:, h], cst["ident"][:, :])
                mm.then_inc(turned, 1)
                pe.wait_ge(k_moved, i + 1)
                pe.wait_ge(v_ready, i + 1)
                for ch in range(2):
                    rows = slice(ch * CHUNK, (ch + 1) * CHUNK)
                    for h in range(HEADS):
                        pe.matmul(p_up[ch][h // 2][:, head_cols(h)], k_tok[rows, h], vt[rows, h * DV:(h + 1) * DV],
                                  start=True, stop=True).then_inc(updated, 1)
                pe.wait_ge(masked, i + 1)
                for h in range(HEADS):
                    out = p_out[h // 2][:, head_cols(h)]
                    vh = vt[:, h * DV:(h + 1) * DV]
                    pe.matmul(out, scores[:, h], vh, start=True, stop=False, skip_group_check=True)
                    pe.matmul(out[0:CHUNK], q_dec[:, h, 0:CHUNK], state[:, 0, h], start=False, stop=False,
                              skip_group_check=True)
                    pe.wait_ge(stated, 2 * HEADS * i + (h + 2))
                    pe.matmul(out[CHUNK:P], q_dec[:, h, CHUNK:P], state[:, 1, h], start=False, stop=True,
                              skip_group_check=True).then_inc(out_done, 1)


def project_rest(nc, w_in, w_conv, h_hi, h_lo, o, inv_rms, y_conv, gates):
    w_view = panel_view(w_in)
    with ExitStack() as ctx:
        def sb(name, shape, dt=F32):
            return ctx.enter_context(nc.sbuf_tensor(f"r_{name}", shape, dt))

        def sem(name):
            return ctx.enter_context(nc.semaphore(f"r_{name}"))

        ring = Ring(nc, ctx, "r_ring")
        taps = sb("taps", [P, CONV_K, KT])
        sig = sb("sig", [P, 2, NP])
        silu = sb("silu", [P, 2, NP])
        cc = sb("cc", [P, BPP, S])
        u = sb("u", [P, BPP, CONV_K - 1 + S])
        y = sb("y", [P, BPP, S])
        gate = sb("gate", [P, 2, BPP, S])
        banks = [ctx.enter_context(nc.psum_tensor(f"r_bank{b}", [P, 512], F32)) for b in range(8)]

        taps_loaded, ready = sem("taps_loaded"), sem("ready")
        sig_done, silu_done, o_done, y_free = sem("sig_done"), sem("silu_done"), sem("o_done"), sem("y_free")
        cc_done, u_done, tap_done, y_done = sem("cc_done"), sem("u_done"), sem("tap_done"), sem("y_done")
        gate_done = sem("gate_done")
        y_stored, gate_stored = sem("y_stored"), [sem(f"gate_stored{s}") for s in range(2)]
        block = ctx.enter_context(nc.Block())

        R0 = 2 * 2 * TT
        C0 = 2 * 3 * PANELS * BPP

        @block.sync
        def _(sp):
            sp.dma_start(taps[:, :, :], w_conv.rearrange("i (b p) -> p i b", p=P),
                         allow_slow_non_contiguous=True).then_inc(taps_loaded, 16)
            cols = [COL_R + NP * n for n in range(PANELS)]
            for n in range(PANELS):
                cols += [COL_CC + NP * n, COL_CX + NP * n, COL_CB + NP * n]
            cols += [COL_GB + NP * n for n in range(PANELS)] + [COL_GA + NP * n for n in range(PANELS)]
            for n, c in enumerate(cols):
                ring.load(sp, n, w_view[:, :, c:c + NP])

        @block.gpsimd
        def _(pool):
            pool.sem_inc(y_free, 1)
            for n in range(PANELS):
                pool.wait_ge(y_done, 4 * (n + 1) + 4)
                pool.dma_start(y_conv[:, n * BPP:(n + 1) * BPP, :], y[:, :, :]).then_inc(y_stored, 16)
                pool.wait_ge(y_stored, 16 * n + 16)
                pool.sem_inc(y_free, 1)
            for n in range(2 * PANELS):
                pool.wait_ge(gate_done, 4 * (n + 1) + 8)
                pool.dma_start(gates[:, n * BPP:(n + 1) * BPP, :], gate[:, n % 2]).then_inc(gate_stored[n % 2], 16)
            pool.wait_ge(y_stored, 16 * PANELS)
            for s in range(2):
                pool.wait_ge(gate_stored[s], 16 * PANELS)

        @block.scalar
        def _(act):
            act.sem_inc(gate_done, 8)
            for s in range(2):
                ring.split_hi(act, s, 0)
            with act.Fori(0, 2) as t:
                for s in range(2):
                    for i in range(TT):
                        r = s * TT + i
                        act.wait_ge(ready, 2 * TT * t + r + 1)
                        act.wait_ge(silu_done, 2 * TT * t + r - 1 + 8)
                        act.activation(sig[:, i % 2], banks[r % len(banks)][:, 0:NP], ACT.Sigmoid).then_inc(sig_done, 1)
                    ring.split_hi(act, s, t + 1)
            with act.Fori(0, PANELS // 2) as t:
                for n in range(6):
                    if n % 3 == 0:
                        for r in range(4):
                            act.wait_ge(ready, R0 + 24 * t + 4 * n + r + 1)
                            act.wait_ge(u_done, 8 * t + 4 * (n // 3) + 4)
                            act.copy(cc[:, r // 2, (r % 2) * HALF:(r % 2 + 1) * HALF],
                                     banks[4 * (n % 2) + r][:, :]) \
                                .then_inc(cc_done, 1)
                    act.wait_ge(ready, R0 + 24 * t + 4 * n + 4)
                    ring.split_hi(act, n % 2, 3 * t + n // 2 + 3)
            for n in range(2 * PANELS):
                for r in range(4):
                    act.wait_ge(ready, R0 + C0 + 4 * n + r + 1)
                    if n >= 2 and r == 0:
                        act.wait_ge(gate_stored[n % 2], 16 * (n // 2))
                    act.activation(gate[:, n % 2, r // 2, (r % 2) * HALF:(r % 2 + 1) * HALF],
                                   banks[4 * (n % 2) + r][:, :], ACT.Sigmoid).then_inc(gate_done, 1)
                if n + 2 < 2 * PANELS:
                    ring.split_hi(act, n % 2, (16 + n) // 2 + 1)

        @block.vector
        def _(dve):
            dve.sem_inc(o_done, 1)
            dve.memset(u[:, :, 0:CONV_K - 1], 0.0).then_inc(u_done, 4)
            dve.sem_inc(silu_done, 8)
            dve.sem_inc(y_done, 4)
            for s in range(2):
                ring.split_lo(dve, s, 0)
            with dve.Fori(0, 2) as t:
                for s in range(2):
                    for i in range(TT):
                        r = s * TT + i
                        dve.wait_ge(sig_done, 2 * TT * t + r + 1)
                        dve.wait_ge(o_done, 1 + 2 * TT * t + r)
                        dve.tensor_tensor(silu[:, i % 2], banks[r % len(banks)][:, 0:NP], sig[:, i % 2],
                                          ALU.mult).then_inc(silu_done, 1)
                        dve.wait_ge(silu_done, 2 * TT * t + r + 1 + 8)
                        o_i = o[:, i, bass.ds(t * 2 * NP + s * NP, NP)]
                        dve.scalar_tensor_tensor(out=o_i, in0=o_i, scalar=inv_rms[:, i, bass.ds(2 * t + s, 1)],
                                                 in1=silu[:, i % 2], op0=ALU.mult, op1=ALU.mult) \
                            .then_inc(o_done, 1)
                    ring.split_lo(dve, s, t + 1)
            dve.wait_ge(taps_loaded, 16)
            with dve.Fori(0, PANELS // 2) as t:
                for n in range(6):
                    if n % 3 == 1:
                        for r in range(4):
                            dve.wait_ge(cc_done, 8 * t + 4 * (n // 3) + r + 1)
                            dve.wait_ge(ready, R0 + 24 * t + 4 * n + r + 1)
                            c = slice((r % 2) * HALF, (r % 2 + 1) * HALF)
                            dve.tensor_tensor(u[:, r // 2, CONV_K - 1 + c.start:CONV_K - 1 + c.stop],
                                              banks[4 * (n % 2) + r][:, :], cc[:, r // 2, c], ALU.mult) \
                                .then_inc(u_done, 1)
                        dve.wait_ge(u_done, 8 * t + 4 * (n // 3) + 4 + 4)
                        dve.wait_ge(y_free, 1 + 2 * t + n // 3)
                        for i in range(CONV_K):
                            for b in range(BPP):
                                block_ = bass.ds(4 * t + 2 * (n // 3) + b, 1)
                                tap = taps[:, i, block_]
                                at = u[:, b, i:i + S]
                                if i == 0:
                                    dve.tensor_scalar(y[:, b], at, tap, None, ALU.mult).then_inc(tap_done, 1)
                                else:
                                    dve.wait_ge(tap_done, 12 * t + 6 * (n // 3) + 2 * (i - 1) + b + 1)
                                    dve.scalar_tensor_tensor(out=y[:, b], in0=at, scalar=tap, in1=y[:, b],
                                                             op0=ALU.mult, op1=ALU.add).then_inc(tap_done, 1)
                    if n % 3 == 2:
                        dve.wait_ge(tap_done, 12 * t + 6 * (n // 3) + 6)
                        for r in range(4):
                            dve.wait_ge(ready, R0 + 24 * t + 4 * n + r + 1)
                            c = slice((r % 2) * HALF, (r % 2 + 1) * HALF)
                            dve.tensor_tensor(y[:, r // 2, c], banks[4 * (n % 2) + r][:, :], y[:, r // 2, c],
                                              ALU.mult).then_inc(y_done, 1)
                    ring.split_lo(dve, n % 2, 3 * t + n // 2 + 3)
            for n in range(2 * PANELS):
                if n + 2 < 2 * PANELS:
                    ring.split_lo(dve, n % 2, (16 + n) // 2 + 1)

        @block.tensor
        def _(pe):
            token_panels(pe, ring, 2, 0, h_hi, h_lo, banks, ready, silu_done, 0)
            pe.wait_ge(silu_done, R0 + 8)
            with pe.Fori(0, PANELS // 2) as t:
                for n in range(6):
                    pe.wait_ge(ring.lo_ready, 6 * t + n + 5)
                    for b in range(BPP):
                        for h in range(2):
                            r = 2 * b + h
                            before = (u_done, y_done, cc_done)[n % 3]
                            pe.wait_ge(before, 8 * t + 4 * (n // 3) + r + 1)
                            c = slice(h * HALF, (h + 1) * HALF)
                            hi, lo = ring.left(n % 2, b)
                            mm = product(pe, banks[4 * (n % 2) + r][:, :], hi, lo,
                                         lambda k: h_hi[:, k, c], lambda k: h_lo[:, k, c])
                            mm.then_inc(ready, 1)
            pe.wait_ge(y_done, 4 * PANELS + 4)
            channel_panels(pe, ring, PANELS, 8, h_hi, h_lo, banks, ready, gate_done, 0)


def branch(nc, name, w, o, y_conv, gates, cst, mix):
    attention = o is not None
    with ExitStack() as ctx:
        def sb(n, shape, dt=F32):
            return ctx.enter_context(nc.sbuf_tensor(f"{name}_{n}", shape, dt))

        def sem(n):
            return ctx.enter_context(nc.semaphore(f"{name}_{n}"))

        ring = Ring(nc, ctx, f"{name}_ring")
        x_hi, x_lo = sb("x_hi", [P, KT, S], F32R), sb("x_lo", [P, KT, S], F32R)
        gate = sb("gate", [P, 2, BPP, S])
        banks = [ctx.enter_context(nc.psum_tensor(f"{name}_bank{b}", [P, 512], F32)) for b in range(RB)]
        if attention:
            turned = [ctx.enter_context(nc.psum_tensor(f"{name}_turned{s}", [P, D], F32)) for s in range(2)]
            part = sb("part", [P, 2, HALF])
        else:
            y = sb("y", [P, 2, S])
        y_loaded = [sem(f"y_loaded{s}") for s in range(2)]
        gate_loaded = [sem(f"gate_loaded{s}") for s in range(2)]
        transposed, hi_done, lo_done = sem("transposed"), sem("hi_done"), sem("lo_done")
        ready, taken, mixed = sem("ready"), sem("taken"), sem("mixed")
        block = ctx.enter_context(nc.Block())

        @block.sync
        def _(sp):
            for n in range(2):
                ring.load(sp, n, panel_view(w)[:, :, n * NP:(n + 1) * NP])
            if not attention:
                for j in range(KT):
                    if j >= 2:
                        sp.wait_ge(lo_done, j - 1)
                    sp.dma_start(y[:, j % 2], y_conv[:, j, :]).then_inc(y_loaded[j % 2], 16)
            for n in range(PANELS):
                if n == 2:
                    for m in range(2, PANELS):
                        ring.load(sp, m, panel_view(w)[:, :, m * NP:(m + 1) * NP])
                if n >= 2:
                    sp.wait_ge(taken, 4 * (n - 1) + RB)
                sp.dma_start(gate[:, n % 2], gates[:, n * BPP:(n + 1) * BPP, :]) \
                    .then_inc(gate_loaded[n % 2], 16)

        @block.scalar
        def _(act):
            ring.split_hi(act, 0, 0)
            for j in range(KT):
                if j == 4:
                    ring.split_hi(act, 1, 0)
                if attention:
                    act.wait_ge(transposed, j + 1)
                    act.copy(x_hi[:, :, j * P:(j + 1) * P],
                             turned[j % 2][:, :].rearrange("p (k c) -> p k c", k=KT)).then_inc(hi_done, 1)
                else:
                    act.wait_ge(y_loaded[j % 2], 16 * (j // 2 + 1))
                    act.copy(x_hi[:, j], y[:, j % 2]).then_inc(hi_done, 1)
            for s in range(2):
                act.wait_ge(ready, 4 * s + 4)
                ring.split_hi(act, s, 1)

        @block.vector
        def _(dve):
            dve.sem_inc(taken, RB)
            ring.split_lo(dve, 0, 0)
            for j in range(KT):
                if j == 4:
                    ring.split_lo(dve, 1, 0)
                dve.wait_ge(hi_done, j + 1)
                if attention:
                    c = slice(j * P, (j + 1) * P)
                    dve.tensor_tensor(x_lo[:, :, c], turned[j % 2][:, :].rearrange("p (k c) -> p k c", k=KT),
                                      f32(x_hi[:, :, c]), ALU.subtract).then_inc(lo_done, 1)
                else:
                    dve.tensor_tensor(x_lo[:, j], y[:, j % 2], f32(x_hi[:, j]),
                                      ALU.subtract).then_inc(lo_done, 1)
            for n in range(PANELS):
                dve.wait_ge(gate_loaded[n % 2], 16 * (n // 2 + 1))
                for r in range(4):
                    k = 4 * n + r
                    dve.wait_ge(ready, k + 1)
                    c = slice((r % 2) * HALF, (r % 2 + 1) * HALF)
                    out = mix[:, n * BPP + r // 2, c]
                    if attention:
                        if k >= 2:
                            dve.wait_ge(mixed, k - 1)
                        dve.tensor_tensor(part[:, k % 2], banks[k % RB][:, :], gate[:, n % 2, r // 2, c],
                                          ALU.mult).then_inc(taken, 1)
                        dve.wait_ge(taken, k + 1 + RB)
                        dve.tensor_tensor(out, part[:, k % 2], out, ALU.add).then_inc(mixed, 1)
                    else:
                        dve.tensor_tensor(out, banks[k % RB][:, :], gate[:, n % 2, r // 2, c],
                                          ALU.mult).then_inc(taken, 1)
                if n < 2:
                    ring.split_lo(dve, n, 1)

        @block.tensor
        def _(pe):
            if attention:
                for i in range(TT):
                    if i >= 2:
                        pe.wait_ge(lo_done, i - 1)
                    for k in range(KT):
                        tr = pe.transpose(turned[i % 2][:, k * P:(k + 1) * P], o[:, i, k * P:(k + 1) * P],
                                          cst["ident"][:, :])
                    tr.then_inc(transposed, 1)
                pe.wait_ge(lo_done, TT)
            channel_panels(pe, ring, 2, 0, x_hi, x_lo, banks, ready, taken, 0,
                           kt_done=None if attention else lo_done)


def project_out(nc, w_out, x, mix, x2):
    with ExitStack() as ctx:
        def sem(n):
            return ctx.enter_context(nc.semaphore(f"o_{n}"))

        ring = Ring(nc, ctx, "o_ring")
        m_hi = ctx.enter_context(nc.sbuf_tensor("o_m_hi", [P, KT, S], F32R))
        m_lo = ctx.enter_context(nc.sbuf_tensor("o_m_lo", [P, KT, S], F32R))
        banks = [ctx.enter_context(nc.psum_tensor(f"o_bank{b}", [P, 512], F32)) for b in range(RB)]
        x_loaded, hi_done, lo_done = sem("x_loaded"), sem("hi_done"), sem("lo_done")
        ready, added = sem("ready"), sem("added")
        block = ctx.enter_context(nc.Block())

        @block.sync
        def _(sp):
            for n in range(PANELS):
                ring.load(sp, n, panel_view(w_out)[:, :, n * NP:(n + 1) * NP])
                if n == 1:
                    sp.dma_start(x2[:, :, :], x.rearrange("(i p) n -> p i n", p=P)).then_inc(x_loaded, 16)

        @block.scalar
        def _(act):
            ring.split_hi(act, 0, 0)
            for j in range(KT):
                if j == 4:
                    ring.split_hi(act, 1, 0)
                act.copy(m_hi[:, j], mix[:, j]).then_inc(hi_done, 1)
            for s in range(2):
                act.wait_ge(ready, TT * (s + 1))
                ring.split_hi(act, s, 1)

        @block.vector
        def _(dve):
            dve.sem_inc(added, RB)
            ring.split_lo(dve, 0, 0)
            for j in range(KT):
                if j == 4:
                    ring.split_lo(dve, 1, 0)
                dve.wait_ge(hi_done, j + 1)
                dve.tensor_tensor(m_lo[:, j], mix[:, j], f32(m_hi[:, j]), ALU.subtract).then_inc(lo_done, 1)
            dve.wait_ge(x_loaded, 16)
            with dve.Fori(0, 2) as t:
                for s in range(2):
                    for i in range(TT):
                        r = s * TT + i
                        dve.wait_ge(ready, 2 * TT * t + r + 1)
                        out = x2[:, i, bass.ds(t * 2 * NP + s * NP, NP)]
                        dve.tensor_tensor(out, banks[r % RB][:, 0:NP], out, ALU.add).then_inc(added, 1)
                    if s == 0:
                        with dve.If(t < 1):
                            ring.split_lo(dve, 0, 1)
                    else:
                        with dve.If(t < 1):
                            ring.split_lo(dve, 1, 1)

        @block.tensor
        def _(pe):
            token_panels(pe, ring, 2, 0, m_hi, m_lo, banks, ready, added, 0, kt_done=lo_done)


def route(nc, x2, g_ffn, w_router, b_router, h_rows, y_rows, cst, rank, gate3, table, row0):
    with ExitStack() as ctx:
        def sb(n, shape, dt=F32):
            return ctx.enter_context(nc.sbuf_tensor(f"g_{n}", shape, dt))

        def sem(n):
            return ctx.enter_context(nc.semaphore(f"g_{n}"))

        junk = sb("junk", [P, D])
        zero = sb("zero", [P, D])
        ht = sb("ht", [P, 2, D])
        hT = sb("hT", [P, 2, KT, P])
        g = sb("g", [P, D])
        wr = sb("wr", [P, KT, E])
        br = sb("br", [P, E])
        stat = sb("stat", [P, 3, TT])
        logits, top = sb("logits", [P, TT, E]), sb("top", [P, TT, 8])
        index, index_f = sb("index", [P, TT, 8], U32), sb("index_f", [P, TT, TOP_K])
        below, expo, gates = (sb(n, [P, TT, TOP_K]) for n in ("below", "expo", "gates"))
        total, inv = sb("total", [P, TT]), sb("inv", [P, TT])
        hot = sb("hot", [P, TT * TOP_K, E])
        chosen = sb("chosen", [P, TT, E], BF16)
        weight = sb("weight", [P, TT, E])
        count, supers = sb("count", [P, E]), sb("supers", [P, E])
        scan = sb("scan", [P, 2, W])
        rows = sb("rows", [P, 8, W])
        cube = sb("cube", [P, W, E])
        rest = sb("rest", [P, TT, E])
        turned = [ctx.enter_context(nc.psum_tensor(f"g_turned{s}", [P, D], F32)) for s in range(2)]
        p_logits = ctx.enter_context(nc.psum_tensor("g_p_logits", [P, 2 * TT, E], F32))
        p_rank = ctx.enter_context(nc.psum_tensor("g_rank", [P, 512], F32))

        loaded, zeroed = sem("loaded"), sem("zeroed")
        squared, rooted, inverted, normed = sem("squared"), sem("rooted"), sem("inverted"), sem("normed")
        transposed, moved, logged = sem("transposed"), sem("moved"), sem("logged")
        chain, maxed, shifted, expd = sem("chain"), sem("maxed"), sem("shifted"), sem("expd")
        picked, ranked = sem("picked"), sem("ranked")
        stored, finished = [sem(f"stored{s}") for s in range(2)], sem("finished")
        block = ctx.enter_context(nc.Block())

        @block.sync
        def _(sp):
            sp.dma_start(g[:, :], g_ffn.partition_broadcast(P)).then_inc(loaded, 16)
            sp.dma_start(br[:, :], b_router.partition_broadcast(P)).then_inc(loaded, 16)
            sp.dma_start(wr[:, :, :], w_router.rearrange("(k p) e -> p k e", p=P)).then_inc(loaded, 16)
            sp.wait_ge(zeroed, 1)
            sp.dma_start(h_rows[S:XROWS, :], zero[:, :]).then_inc(finished, 16)
            sp.dma_start(y_rows[S:XROWS, :], zero[:, :]).then_inc(finished, 16)
            sp.dma_start(y_rows[0:S, :].rearrange("(i p) n -> p i n", p=P), x2[:, :, :]).then_inc(finished, 16)
            for i in range(TT):
                sp.wait_ge(normed, i + 1)
                sp.dma_start(h_rows[i * P:(i + 1) * P, :], ht[:, i % 2]).then_inc(stored[i % 2], 16)
            sp.wait_ge(finished, 48)
            for s in range(2):
                sp.wait_ge(stored[s], 16 * TT // 2)

        @block.scalar
        def _(act):
            for i in range(TT):
                if i:
                    act.wait_ge(squared, i)
                act.activation(junk[:, :], x2[:, i], ACT.Square,
                               accum_out=stat[:, 0, i:i + 1]).then_inc(squared, 1)
            act.wait_ge(squared, TT)
            act.activation(stat[:, 1, :], stat[:, 0, :], ACT.Sqrt, bias=cst["eps"][:, :],
                           scale=1.0 / D).then_inc(rooted, 1)
            for i in range(TT):
                act.wait_ge(transposed, i + 1)
                if i >= 2:
                    act.wait_ge(logged, i - 1)
                act.copy(hT[:, i % 2].rearrange("p k c -> p (k c)"), turned[i % 2][:, :]).then_inc(moved, 1)
            act.wait_ge(shifted, 1)
            act.activation(expo[:, :, :], below[:, :, :], ACT.Exp).then_inc(expd, 1)

        @block.vector
        def _(dve):
            dve.memset(zero[:, :], 0.0).then_inc(zeroed, 1)
            dve.wait_ge(loaded, 48)
            dve.wait_ge(rooted, 1)
            dve.reciprocal(stat[:, 2, :], stat[:, 1, :]).then_inc(inverted, 1)
            dve.wait_ge(inverted, 1)
            for i in range(TT):
                if i >= 2:
                    dve.wait_ge(transposed, i - 1)
                    dve.wait_ge(stored[i % 2], 16 * (i // 2))
                dve.scalar_tensor_tensor(out=ht[:, i % 2], in0=x2[:, i], scalar=stat[:, 2, i:i + 1],
                                         in1=g[:, :], op0=ALU.mult, op1=ALU.mult).then_inc(normed, 1)
            done = 0

            def step(ins):
                nonlocal done
                done += 1
                ins.then_inc(chain, 1)
                dve.wait_ge(chain, done)

            dve.wait_ge(logged, TT)
            step(dve.tensor_tensor(logits[:, :, :], p_logits[:, 0:TT],
                                   br[:, :].unsqueeze(1).to_broadcast([P, TT, E]), ALU.add))
            for i in range(TT):
                dve.max(top[:, i], logits[:, i]).then_inc(maxed, 1)
            dve.wait_ge(maxed, TT)
            dve.tensor_tensor(below[:, :, :], top[:, :, 0:TOP_K], top[:, :, 0:1].to_broadcast([P, TT, TOP_K]),
                              ALU.subtract).then_inc(shifted, 1)
            for i in range(TT):
                dve.max_index(index[:, i], top[:, i], logits[:, i]).then_inc(maxed, 1)
            dve.wait_ge(maxed, 2 * TT)
            step(dve.tensor_copy(index_f[:, :, :], index[:, :, 0:TOP_K]))
            wide = [P, TT * TOP_K, E]
            step(dve.tensor_tensor(hot[:, :, :], cst["iota"][:, 0:E].unsqueeze(1).to_broadcast(wide),
                                   index_f[:, :, :].rearrange("p i k -> p (i k)").unsqueeze(2).to_broadcast(wide),
                                   ALU.is_equal))
            by_expert = hot[:, :, :].rearrange("p (i k) e -> p i e k", k=TOP_K)
            with nc.allow_low_precision(reason="sums of one 1 and zeros"):
                dve.tensor_reduce(chosen[:, :, :], by_expert, AX.X, ALU.add).then_inc(picked, 1)
            dve.wait_ge(picked, 1)
            dve.wait_ge(expd, 1)
            step(dve.tensor_reduce(total[:, :], expo[:, :, :], AX.X, ALU.add))
            step(dve.reciprocal(inv[:, :], total[:, :]))
            step(dve.tensor_tensor(gates[:, :, :], expo[:, :, :],
                                   inv[:, :].unsqueeze(2).to_broadcast([P, TT, TOP_K]), ALU.mult))
            step(dve.tensor_tensor(hot[:, :, :], hot[:, :, :],
                                   gates[:, :, :].rearrange("p i k -> p (i k)").unsqueeze(2).to_broadcast(wide),
                                   ALU.mult))
            step(dve.tensor_reduce(weight[:, :, :], by_expert, AX.X, ALU.add))
            dve.wait_ge(ranked, 1)
            pos = p_rank[:, 0:TT * E].rearrange("p (i e) -> p i e", i=TT)
            step(dve.scalar_tensor_tensor(out=rest[:, :, :], in0=pos, scalar=-NPOS, in1=chosen[:, :, :],
                                          op0=ALU.add, op1=ALU.mult))
            step(dve.tensor_scalar(rank[:, :, :], rest[:, :, :], NPOS, None, ALU.add))
            step(dve.tensor_copy(gate3[:, :, :, 0], weight[:, :, :]))
            step(dve.tensor_tensor(rest[:, :, :], weight[:, :, :], gate3[:, :, :, 0], ALU.subtract))
            step(dve.tensor_copy(gate3[:, :, :, 1], rest[:, :, :]))
            step(dve.tensor_tensor(weight[:, :, :], rest[:, :, :], gate3[:, :, :, 1], ALU.subtract))
            step(dve.tensor_copy(gate3[:, :, :, 2], weight[:, :, :]))
            step(dve.tensor_copy(count[:, :], p_rank[:, TT * E:(TT + 1) * E]))
            step(dve.tensor_scalar(supers[:, :], count[:, :], 0.0, None, ALU.is_gt))
            for m in range(SUPER, S, SUPER):
                step(dve.scalar_tensor_tensor(out=supers[:, :], in0=count[:, :], scalar=float(m),
                                              in1=supers[:, :], op0=ALU.is_gt, op1=ALU.add))

            def running_sum(src, width):
                step(dve.tensor_copy(scan[:, 0, 0:width], src))
                a, sh = 0, 1
                while sh < width:
                    step(dve.tensor_copy(scan[:, 1 - a, 0:sh], scan[:, a, 0:sh]))
                    step(dve.tensor_tensor(scan[:, 1 - a, sh:width], scan[:, a, sh:width],
                                           scan[:, a, 0:width - sh], ALU.add))
                    a, sh = 1 - a, 2 * sh
                return scan[:, a, 0:width]

            upto = running_sum(supers[:, :], E)
            number = cst["iota"][:, 0:W]
            wide = [P, W, E]
            expert, start, held, part, live, second, seconds, spare = (rows[:, r] for r in range(8))
            step(dve.tensor_tensor(cube[:, :, :], upto.unsqueeze(1).to_broadcast(wide),
                                   number.unsqueeze(2).to_broadcast(wide), ALU.is_le))
            step(dve.tensor_reduce(expert, cube[:, :, :], AX.X, ALU.add))
            step(dve.tensor_scalar(expert, expert, float(E - 1), None, ALU.min))
            step(dve.tensor_tensor(cube[:, :, :], cube[:, :, :],
                                   supers[:, :].unsqueeze(1).to_broadcast(wide), ALU.mult))
            step(dve.tensor_reduce(start, cube[:, :, :], AX.X, ALU.add))
            step(dve.tensor_tensor(part, number, start, ALU.subtract))
            step(dve.tensor_scalar(row0[:, :], part, float(SUPER), None, ALU.mult))
            step(dve.tensor_tensor(cube[:, :, :], cst["iota"][:, 0:E].unsqueeze(1).to_broadcast(wide),
                                   expert.unsqueeze(2).to_broadcast(wide), ALU.is_equal))
            step(dve.tensor_tensor(cube[:, :, :], cube[:, :, :],
                                   count[:, :].unsqueeze(1).to_broadcast(wide), ALU.mult))
            step(dve.tensor_reduce(held, cube[:, :, :], AX.X, ALU.add))
            step(dve.tensor_tensor(held, held, row0[:, :], ALU.subtract))
            step(dve.tensor_scalar(live, number, upto[:, E - 1:E], None, ALU.is_lt))
            step(dve.scalar_tensor_tensor(out=second, in0=held, scalar=float(P), in1=live, op0=ALU.is_gt,
                                          op1=ALU.mult))
            step(dve.tensor_copy(table[:, 3, 0:1], upto[:, E - 1:E]))
            total_seconds = running_sum(second, W)
            step(dve.tensor_tensor(seconds, total_seconds, second, ALU.subtract))
            step(dve.tensor_copy(table[:, 0], expert))
            step(dve.tensor_copy(table[:, 1], second))
            step(dve.tensor_copy(table[:, 2], seconds))

        @block.tensor
        def _(pe):
            pe.wait_ge(loaded, 48)

            def logit(i):
                pe.wait_ge(moved, i + 1)
                for k in range(KT):
                    mm = pe.matmul(p_logits[:, i], hT[:, i % 2, k], wr[:, k], start=(k == 0),
                                   stop=(k == KT - 1))
                mm.then_inc(logged, 1)

            for i in range(TT):
                pe.wait_ge(normed, i + 1)
                if i >= 2:
                    pe.wait_ge(moved, i - 1)
                for k in range(KT):
                    tr = pe.transpose(turned[i % 2][:, k * P:(k + 1) * P], ht[:, i % 2, k * P:(k + 1) * P],
                                      cst["ident"][:, :])
                tr.then_inc(transposed, 1)
                if i:
                    logit(i - 1)
            logit(TT - 1)
            pe.wait_ge(picked, 1)
            for i in range(TT + 1):
                out = p_rank[:, i * E:(i + 1) * E]
                for j in range(i):
                    mm = pe.matmul(out, cst["ones16"][:, :], chosen[:, j], start=(j == 0),
                                   stop=(j == TT - 1))
                if i < TT:
                    mm = pe.matmul(out, cst["before"][:, :], chosen[:, i], start=(i == 0), stop=True)
            mm.then_inc(ranked, 1)


def experts(nc, w_gate_up, b_gate_up, w_down, b_down, h_rows, y_rows, cst, rank, gate3, table, row0):
    gu_view = w_gate_up.rearrange("e (k p) n -> e p k n", p=P)
    dn_view = w_down.rearrange("e (k p) n -> e p k n", p=P)
    with ExitStack() as ctx:
        def sb(n, shape, dt=F32):
            return ctx.enter_context(nc.sbuf_tensor(f"m_{n}", shape, dt))

        signals = []

        def sem(n):
            signals.append(ctx.enter_context(nc.semaphore(f"m_{n}")))
            return signals[-1]

        def two(n):
            return [sem(f"{n}{x}") for x in range(2)]

        def psum(n):
            return ctx.enter_context(nc.psum_tensor(f"m_{n}", [P, 512], F32))

        raw = sb("raw", [P, RS, KP, NW])
        w_hi, w_lo = sb("w_hi", [P, WS, KP, NW], F32R), sb("w_lo", [P, WS, KP, NW], F32R)
        xg = sb("xg", [P, 2, D])
        x_hi, x_lo = sb("x_hi", [P, 2, KT, P], F32R), sb("x_lo", [P, 2, KT, P], F32R)
        a_hi, a_lo = sb("a_hi", [P, 2, KT, P], F32R), sb("a_lo", [P, 2, KT, P], F32R)
        y_out = sb("y_out", [P, 2, D])
        b_raw, b_split = sb("b_raw", [P, F]), sb("b_split", [P, 2 * F], F32R)
        pick = sb("pick", [P, 2, P], F32R)
        gate_t, act_t = sb("gate_t", [P, 2, NW]), sb("act_t", [P, 2, NW])
        place = sb("place", [P, TT])
        hits = sb("hits", [P, TT, SUPER], BF16)
        found = sb("found", [P, 2, 6])
        looked = sb("looked", [P, 2, 3])
        slot_next, slot_now = sb("slot_next", [P, 2], I32), sb("slot_now", [P, 2], I32)
        weight_next, weight_now = sb("weight_next", [P, 2]), sb("weight_now", [P, 2])
        pg = [[psum(f"pg{x}{b}") for b in range(2)] for x in range(2)]
        turn = [psum(f"turn{x}") for x in range(2)]
        p_found = psum("found_p")

        raw_loaded = [sem(f"raw_loaded{s}") for s in range(RS)]
        whi, wlo = sem("whi"), sem("wlo")
        bg_loaded, bg_hi, bg_lo = sem("bg_loaded"), sem("bg_hi"), sem("bg_lo")
        bd_loaded, bd_hi, bd_lo = sem("bd_loaded"), sem("bd_hi"), sem("bd_lo")
        prod = two("prod")
        clipped, taken, gated = two("clipped"), two("taken"), two("gated")
        sig, activated = two("sig"), two("activated")
        turned, ahi, alo = two("turned"), two("ahi"), two("alo")
        x_turned, xhi, xlo = two("x_turned"), two("xhi"), two("xlo")
        y_done, scattered = two("y_done"), two("scattered")
        gathered, added = ([ctx.enter_context(nc.semaphore(f"m_{n}{x}")) for x in range(2)]
                           for n in ("gathered", "added"))
        placed, hit, counted = sem("placed"), sem("hit"), sem("counted")
        look, look_step, current = sem("look"), sem("look_step"), sem("current")
        waits_met = sem("waits_met")
        rows_in = sem("rows_in")
        LOOKS = 5
        bias_cleared, split_cleared = sem("bias_cleared"), sem("split_cleared")
        for signal in signals:
            nc.gpsimd.sem_inc(signal, OPEN)
        nc.all_engine_barrier()
        block = ctx.enter_context(nc.Block())

        def load_value(eng, row, at, high):
            return eng.value_load(table[0:1, row, bass.ds(at, 1)], min_val=0, max_val=high)

        def per_tile(eng, t, nb, hb, body):
            body(0, t)
            with eng.If(hb > 0):
                body(1, nb)

        def seen(eng, sems, each, t, nb, hb, k):
            eng.wait_ge(sems[0], each * t + (OPEN + k))
            eng.wait_ge(sems[1], each * nb + k * hb + OPEN)

        @block.sync
        def _(sp):
            supers = load_value(sp, 3, 0, MAX_SUPERS)

            def panel(m, e, g):
                if not (isinstance(g, int) and g + m < RS):
                    sp.wait_ge(wlo, g + (OPEN + m - RS + 1))
                if m < GU:
                    c, k = (m // 2 % 2) * F + (m // 4) * NW, (m % 2) * KP
                    src = gu_view[bass.ds(e, 1), :, k:k + KP, c:c + NW]
                else:
                    c, k = (m % 2) * NW, ((m - GU) // 2) * KP
                    src = dn_view[bass.ds(e, 1), :, k:k + KP, c:c + NW]
                sp.dma_start(raw[:, m % RS], src.rearrange("a p k n -> p (a k) n")) \
                    .then_inc(raw_loaded[m % RS], 16)

            def gate_bias(e):
                for half in range(2):
                    for row in (32 * half, 64 + 32 * half):
                        sp.dma_start(b_raw[row:row + 1, :], b_gate_up[bass.ds(e, 1), half * F:(half + 1) * F]) \
                            .then_inc(bg_loaded, 16)

            e = load_value(sp, 0, 0, E - 1)
            sp.wait_ge(bias_cleared, OPEN + 1)
            gate_bias(e)
            for m in range(AHEAD):
                panel(m, e, 0)
            with sp.Fori(0, supers) as t:
                e = load_value(sp, 0, t, E - 1)
                sp.wait_ge(bg_lo, t + (OPEN + 1))
                for row in (0, 64):
                    sp.dma_start(b_raw[row:row + 1, :], b_down[bass.ds(e, 1), :]).then_inc(bd_loaded, 16)
                for m in range(AHEAD, MP):
                    panel(m, e, MP * t)
                e = load_value(sp, 0, t + 1, E - 1)
                for m in range(AHEAD):
                    if m == 3:
                        sp.wait_ge(bd_lo, t + (OPEN + 1))
                        gate_bias(e)
                    panel(m, e, MP * t + MP)

        @block.gpsimd
        def _(pool):
            pool.memset(b_raw[:, :], 0.0).then_inc(bias_cleared, 1)
            supers = load_value(pool, 3, 0, MAX_SUPERS)

            def lookup(t, n):
                e = load_value(pool, 0, t, E - 1)
                pool.wait_ge(counted, OPEN + n)
                pool.tensor_tensor(place[:, :], rank[:, :, bass.ds(e, 1)].rearrange("p i a -> p (i a)"),
                                   row0[:, bass.ds(t, 1)].to_broadcast([P, TT]), ALU.subtract) \
                    .then_inc(placed, 1)
                pool.wait_ge(placed, n + (OPEN + 1))
                pool.sem_inc(waits_met, 1)
                for i in range(TT):
                    last = pool.tensor_scalar(hits[:, i], cst["iota"][:, :], place[:, i:i + 1], None,
                                              ALU.is_equal)
                last.then_inc(hit, 1)

            def gather(n, second, before):
                pool.wait_ge(look, n + (OPEN + 1))
                pool.sem_inc(waits_met, 1)

                def rows(x):
                    pool.indirect_dma_start(out=xg[:, x, :], out_offset=None, in_=h_rows[:, :],
                                            in_offset=bass.IndirectOffsetOnAxis(ap=slot_next[:, x:x + 1], axis=0)) \
                        .then_inc(gathered[x], 16)

                rows(0)
                with pool.If(second > 0):
                    rows(1)
                pool.wait_ge(gathered[0], 16 * n + 16)
                pool.sem_inc(waits_met, 1)
                with pool.If(second > 0):
                    pool.wait_ge(gathered[1], 16 * before + 16)
                    pool.sem_inc(waits_met, 1)
                pool.sem_inc(rows_in, 1)

            lookup(0, 0)
            gather(0, load_value(pool, 1, 0, 1), 0)
            lookup(1, 1)
            with pool.Fori(0, supers) as t:
                hb = load_value(pool, 1, t, 1)
                nb = load_value(pool, 2, t, MAX_SUPERS)
                pool.wait_ge(x_turned[0], t + (OPEN + 1))
                pool.wait_ge(x_turned[1], OPEN + nb + hb)
                gather(t + 1, load_value(pool, 1, t + 1, 1), nb + hb)
                lookup(t + 2, t + 2)

                def scatter(x, n):
                    pool.wait_ge(y_done[x], OPEN + 2 * n + 2)
                    pool.wait_ge(current, t + (OPEN + 1))
                    pool.sem_inc(waits_met, 1)
                    pool.indirect_dma_start(out=y_rows[:, :],
                                            out_offset=bass.IndirectOffsetOnAxis(ap=slot_now[:, x:x + 1], axis=0),
                                            in_=y_out[:, x, :], in_offset=None, compute_op=ALU.add) \
                        .then_inc(added[x], 16)
                    pool.wait_ge(added[x], 16 * n + 16)
                    pool.sem_inc(scattered[x], 1)

                per_tile(pool, t, nb, hb, scatter)

        @block.scalar
        def _(act):
            supers = load_value(act, 3, 0, MAX_SUPERS)

            def split(m, t):
                act.wait_ge(raw_loaded[m % RS], 16 * (MP // RS) * t + (OPEN + 16 * (m // RS) + 16))
                act.copy(w_hi[:, m % WS], raw[:, m % RS]).then_inc(whi, 1)

            def gate_bias(n):
                act.wait_ge(bg_loaded, OPEN + 64 * n + 64)
                act.copy(b_split[:, 0:F], b_raw[:, :]).then_inc(bg_hi, 1)

            def x_split(x, n):
                act.wait_ge(x_turned[x], n + (OPEN + 1))
                act.copy(x_hi[:, x, 0:4].rearrange("p k c -> p (k c)"), turn[0][:, :])
                act.copy(x_hi[:, x, 4:8].rearrange("p k c -> p (k c)"), turn[1][:, :]).then_inc(xhi[x], 1)

            act.wait_ge(bias_cleared, OPEN + 1)
            act.wait_ge(split_cleared, OPEN + 1)
            gate_bias(0)
            for m in range(AHEAD):
                if m == 2:
                    x_split(0, 0)
                split(m, 0)
            with act.If(load_value(act, 1, 0, 1) > 0):
                x_split(1, 0)
            with act.Fori(0, supers) as t:
                hb = load_value(act, 1, t, 1)
                nb = load_value(act, 2, t, MAX_SUPERS)
                hb_next = load_value(act, 1, t + 1, 1)

                def sigmoid(j):
                    def body(x, n):
                        act.wait_ge(clipped[x], 2 * n + (OPEN + j + 1))
                        act.activation(act_t[:, x], gate_t[:, x], ACT.Sigmoid, scale=ALPHA).then_inc(sig[x], 1)
                    per_tile(act, t, nb, hb, body)

                def a_split(j):
                    def body(x, n):
                        act.wait_ge(turned[x], 2 * n + (OPEN + j + 1))
                        act.copy(a_hi[:, x, KP * j:KP * (j + 1)].rearrange("p k c -> p (k c)"), turn[x][:, :]) \
                            .then_inc(ahi[x], 1)
                    per_tile(act, t, nb, hb, body)

                def store_y(b):
                    def body(x, n):
                        act.wait_ge(prod[x], MP * n + (OPEN + MP - 1 + b))
                        act.wait_ge(current, t + (OPEN + 1))
                        act.activation(y_out[:, x, b * 512:(b + 1) * 512], pg[x][b][:, :], ACT.Copy,
                                       scale=weight_now[:, x:x + 1]).then_inc(y_done[x], 1)
                    per_tile(act, t, nb, hb, body)

                for m in range(MP):
                    seen(act, prod, MP, t, nb, hb, m + 1)
                    if m in (2, 6):
                        sigmoid(m // 4)
                    if m in (5, 9):
                        a_split(m // 8)
                    if m == 7:
                        x_split(0, t + 1)
                    if m >= 10:
                        store_y(m - 10)
                    split((m + AHEAD) % MP, t + (m + AHEAD) // MP)
                    if m == 3:
                        act.wait_ge(bd_loaded, OPEN + 32 * t + 32)
                        act.copy(b_split[:, F:2 * F], b_raw[:, :]).then_inc(bd_hi, 1)
                    if m == 8:
                        gate_bias(t + 1)
                with act.If(hb_next > 0):
                    x_split(1, nb + hb)

        @block.vector
        def _(dve):
            dve.memset(f32(b_split[:, :]), 0.0)
            dve.memset(f32(pick[:, :, :]), 0.0).then_inc(split_cleared, 1)
            supers = load_value(dve, 3, 0, MAX_SUPERS)
            dve.wait_ge(bias_cleared, OPEN + 1)
            dve.wait_ge(split_cleared, OPEN + 1)
            for x in range(2):
                for row in (32 * x, 64 + 32 * x):
                    dve.memset(f32(pick[row:row + 1, x, :]), 1.0)

            def split(m, g):
                dve.wait_ge(whi, g + (OPEN + m + 1))
                dve.tensor_tensor(w_lo[:, m % WS], raw[:, m % RS], f32(w_hi[:, m % WS]),
                                  ALU.subtract).then_inc(wlo, 1)

            def bias(cols, hi, lo, n):
                dve.wait_ge(hi, n + (OPEN + 1))
                dve.tensor_tensor(b_split[64:97, cols], b_raw[64:97, :], f32(b_split[64:97, cols]),
                                  ALU.subtract).then_inc(lo, 1)

            def x_split(x, n):
                dve.wait_ge(xhi[x], n + (OPEN + 1))
                dve.tensor_tensor(x_lo[:, x, 0:4].rearrange("p k c -> p (k c)"), turn[0][:, :],
                                  f32(x_hi[:, x, 0:4].rearrange("p k c -> p (k c)")), ALU.subtract)
                dve.tensor_tensor(x_lo[:, x, 4:8].rearrange("p k c -> p (k c)"), turn[1][:, :],
                                  f32(x_hi[:, x, 4:8].rearrange("p k c -> p (k c)")),
                                  ALU.subtract).then_inc(xlo[x], 1)

            def read_slots(n):
                dve.wait_ge(counted, n + (OPEN + 1))
                k = LOOKS * n

                def step(ins, last=False):
                    nonlocal k
                    k = k + 1
                    if last:
                        ins.then_inc(look, 1)
                    else:
                        ins.then_inc(look_step, 1)
                        dve.wait_ge(look_step, OPEN + k)

                step(dve.tensor_copy(found[:, :, :], p_found[:, 0:12].rearrange("p (x c) -> p x c", x=2)))
                step(dve.tensor_tensor(looked[:, :, 0], found[:, :, 0], found[:, :, 1], ALU.add))
                step(dve.scalar_tensor_tensor(out=looked[:, :, 1], in0=found[:, :, 2],
                                              scalar=cst["spare"][:, 1:2], in1=looked[:, :, 0],
                                              op0=ALU.mult, op1=ALU.add))
                step(dve.tensor_tensor(looked[:, :, 2], found[:, :, 3], found[:, :, 4], ALU.add))
                step(dve.tensor_tensor(weight_next[:, :], looked[:, :, 2], found[:, :, 5], ALU.add))
                step(dve.tensor_scalar(slot_next[:, :], looked[:, :, 1], cst["spare"][:, 0:1], None, ALU.add),
                     last=True)

            read_slots(0)
            bias(slice(0, F), bg_hi, bg_lo, 0)
            for m in range(AHEAD):
                if m == 2:
                    x_split(0, 0)
                split(m, 0)
            with dve.If(load_value(dve, 1, 0, 1) > 0):
                x_split(1, 0)
            with dve.Fori(0, supers) as t:
                hb = load_value(dve, 1, t, 1)
                nb = load_value(dve, 2, t, MAX_SUPERS)
                hb_next = load_value(dve, 1, t + 1, 1)

                def clip_gate(j):
                    def body(x, n):
                        dve.wait_ge(prod[x], MP * n + (OPEN + 4 * j + 2))
                        dve.wait_ge(activated[x], 2 * n + (OPEN + j))
                        dve.tensor_scalar(gate_t[:, x], pg[x][0][:, :], LIMIT, None, ALU.min) \
                            .then_inc(clipped[x], 1)
                    per_tile(dve, t, nb, hb, body)

                def activate(j):
                    def body(x, n):
                        dve.wait_ge(sig[x], 2 * n + (OPEN + j + 1))
                        dve.tensor_tensor(act_t[:, x], gate_t[:, x], act_t[:, x], ALU.mult).then_inc(gated[x], 1)
                        dve.wait_ge(gated[x], 2 * n + (OPEN + j + 1))
                        dve.wait_ge(prod[x], MP * n + (OPEN + 4 * j + 4))
                        dve.tensor_scalar(gate_t[:, x], pg[x][1][:, :], LIMIT, -LIMIT, ALU.min, ALU.max) \
                            .then_inc(taken[x], 1)
                        dve.wait_ge(taken[x], 2 * n + (OPEN + j + 1))
                        dve.scalar_tensor_tensor(out=act_t[:, x], in0=gate_t[:, x], scalar=1.0,
                                                 in1=act_t[:, x], op0=ALU.add, op1=ALU.mult) \
                            .then_inc(activated[x], 1)
                    per_tile(dve, t, nb, hb, body)

                def a_split(j):
                    def body(x, n):
                        dve.wait_ge(ahi[x], 2 * n + (OPEN + j + 1))
                        k = slice(KP * j, KP * (j + 1))
                        dve.tensor_tensor(a_lo[:, x, k].rearrange("p k c -> p (k c)"), turn[x][:, :],
                                          f32(a_hi[:, x, k].rearrange("p k c -> p (k c)")), ALU.subtract) \
                            .then_inc(alo[x], 1)
                    per_tile(dve, t, nb, hb, body)

                for m in range(MP):
                    if m in (1, 5):
                        clip_gate(m // 4)
                    if m in (3, 7):
                        activate(m // 4)
                    if m == 3:
                        dve.wait_ge(y_done[0], OPEN + 2 * t)
                        dve.wait_ge(y_done[1], OPEN + 2 * nb)
                        dve.wait_ge(scattered[0], OPEN + t)
                        dve.wait_ge(scattered[1], OPEN + nb)
                        dve.tensor_copy(weight_now[:, :], weight_next[:, :])
                        dve.tensor_copy(slot_now[:, :], slot_next[:, :]).then_inc(current, 1)
                        dve.wait_ge(rows_in, t + (OPEN + 1))
                        read_slots(t + 1)
                    if m in (5, 9):
                        a_split(m // 8)
                    if m == 8:
                        x_split(0, t + 1)
                    split((m + AHEAD) % MP, MP * (t + (m + AHEAD) // MP))
                    if m == 4:
                        bias(slice(F, 2 * F), bd_hi, bd_lo, t)
                    if m == 9:
                        bias(slice(0, F), bg_hi, bg_lo, t + 1)
                with dve.If(hb_next > 0):
                    x_split(1, nb + hb)

        @block.tensor
        def _(pe):
            supers = load_value(pe, 3, 0, MAX_SUPERS)

            def find(n, e):
                pe.wait_ge(hit, n + (OPEN + 1))
                pe.wait_ge(look, OPEN + n)
                for x in range(2):
                    for src, c in ((lambda i: cst["tokens"][:, i, :], 0),
                                   (lambda i: gate3[:, i, bass.ds(e, 1), :].rearrange("p a c -> p (a c)"), 3)):
                        for i in range(TT):
                            mm = pe.matmul(p_found[:, 6 * x + c:6 * x + c + 3],
                                           hits[:, i, x * P:(x + 1) * P], src(i), start=(i == 0),
                                           stop=(i == TT - 1))
                mm.then_inc(counted, 1)

            def x_turn(x, n):
                for k in range(KT):
                    tr = pe.transpose(turn[k // 4][:, (k % 4) * P:(k % 4 + 1) * P], xg[:, x, k * P:(k + 1) * P],
                                      cst["ident"][:, :])
                tr.then_inc(x_turned[x], 1)

            find(0, load_value(pe, 0, 0, E - 1))
            pe.wait_ge(rows_in, OPEN + 1)
            x_turn(0, 0)
            with pe.If(load_value(pe, 1, 0, 1) > 0):
                pe.wait_ge(xlo[0], OPEN + 1)
                x_turn(1, 0)
            with pe.Fori(0, supers) as t:
                hb = load_value(pe, 1, t, 1)
                nb = load_value(pe, 2, t, MAX_SUPERS)
                hb_next = load_value(pe, 1, t + 1, 1)
                e_next = load_value(pe, 0, t + 1, E - 1)

                def panel(m):
                    down, bank = m >= GU, (m % 2 if m >= GU else m // 2 % 2)
                    kh = (m - GU) // 2 if down else m % 2

                    def body(x, n):
                        out = pg[x][bank][:, :]
                        if m == 0:
                            pe.wait_ge(xlo[x], n + (OPEN + 1))
                        if m in (0, 2):
                            pe.wait_ge(y_done[x], 2 * n + (OPEN - 1 + bank))
                        elif kh == 0:
                            pe.wait_ge(taken[x] if bank else clipped[x], 2 * n + (OPEN + m // 4))
                        if down:
                            pe.wait_ge(alo[x], 2 * n + (OPEN + kh + 1))
                        if kh == 0:
                            c = F + bank * NW if down else m // 4 * NW
                            pe.matmul(out, pick[:, 0 if down else bank, :], b_split[:, c:c + NW], start=True,
                                      stop=False, skip_group_check=True)
                        lh, ll = (a_hi, a_lo) if down else (x_hi, x_lo)
                        product(pe, out, lambda k: lh[:, x, KP * kh + k], lambda k: ll[:, x, KP * kh + k],
                                lambda k: w_hi[:, m % WS, k], lambda k: w_lo[:, m % WS, k],
                                first=False, last=(kh == 1), kts=range(KP)).then_inc(prod[x], 1)

                    pe.wait_ge(wlo, MP * t + (OPEN + m + 1))
                    if m == 0:
                        pe.wait_ge(bg_lo, t + (OPEN + 1))
                    if m == GU:
                        pe.wait_ge(bd_lo, t + (OPEN + 1))
                    per_tile(pe, t, nb, hb, body)

                def a_turn(j):
                    def body(x, n):
                        pe.wait_ge(activated[x], 2 * n + (OPEN + j + 1))
                        pe.wait_ge(alo[x], 2 * n + (OPEN + j))
                        for b in range(KP):
                            tr = pe.transpose(turn[x][:, b * P:(b + 1) * P], act_t[:, x, b * P:(b + 1) * P],
                                              cst["ident"][:, :])
                        tr.then_inc(turned[x], 1)
                    per_tile(pe, t, nb, hb, body)

                for m in range(MP):
                    panel(m)
                    if m == 1:
                        find(t + 1, e_next)
                    if m == 5:
                        a_turn(0)
                    if m == 7:
                        pe.wait_ge(rows_in, t + (OPEN + 2))
                        seen(pe, alo, 2, t, nb, hb, 1)
                        x_turn(0, t + 1)
                    if m == 9:
                        pe.wait_ge(xlo[0], t + (OPEN + 2))
                        a_turn(1)
                with pe.If(hb_next > 0):
                    seen(pe, alo, 2, t, nb, hb, 2)
                    x_turn(1, nb + hb)


def finish(nc, y_rows, g_final, out, cst):
    with ExitStack() as ctx:
        def sb(n, shape, dt=F32):
            return ctx.enter_context(nc.sbuf_tensor(f"f_{n}", shape, dt))

        def sem(n):
            return ctx.enter_context(nc.semaphore(f"f_{n}"))

        yt, junk, ot, g = sb("yt", [P, TT, D]), sb("junk", [P, 2, D]), sb("ot", [P, TT, D]), sb("g", [P, D])
        stat = sb("stat", [P, 3, TT])
        loaded, g_loaded = [sem(f"loaded{i}") for i in range(TT)], sem("g_loaded")
        squared, rooted, inverted, normed, stored = (sem("squared"), sem("rooted"), sem("inverted"),
                                                     sem("normed"), sem("stored"))
        block = ctx.enter_context(nc.Block())

        @block.sync
        def _(sp):
            for i in range(TT):
                sp.dma_start(yt[:, i], y_rows[i * P:(i + 1) * P, :]).then_inc(loaded[i], 16)
                if i == 0:
                    sp.dma_start(g[:, :], g_final.partition_broadcast(P)).then_inc(g_loaded, 16)
            for i in range(TT):
                sp.wait_ge(normed, i + 1)
                sp.dma_start(out[i * P:(i + 1) * P, :], ot[:, i]).then_inc(stored, 16)
            sp.wait_ge(stored, 16 * TT)

        @block.scalar
        def _(act):
            for i in range(TT):
                act.wait_ge(loaded[i], 16)
                if i >= 2:
                    act.wait_ge(squared, i - 1)
                act.activation(junk[:, i % 2], yt[:, i], ACT.Square,
                               accum_out=stat[:, 0, i:i + 1]).then_inc(squared, 1)
                act.wait_ge(squared, i + 1)
                act.activation(stat[:, 1, i:i + 1], stat[:, 0, i:i + 1], ACT.Sqrt, bias=cst["eps"][:, :],
                               scale=1.0 / D).then_inc(rooted, 1)

        @block.vector
        def _(dve):
            dve.wait_ge(g_loaded, 16)
            for i in range(TT):
                dve.wait_ge(rooted, i + 1)
                dve.reciprocal(stat[:, 2, i:i + 1], stat[:, 1, i:i + 1]).then_inc(inverted, 1)
                dve.wait_ge(inverted, i + 1)
                dve.scalar_tensor_tensor(out=ot[:, i], in0=yt[:, i], scalar=stat[:, 2, i:i + 1], in1=g[:, :],
                                         op0=ALU.mult, op1=ALU.mult).then_inc(normed, 1)


def clear_signals(nc):
    nc.all_engine_barrier()
    used = set(nc.released_uncleared_semaphores)
    for first in sorted(n for n in used if n - 1 not in used):
        stop = first
        while stop in used:
            stop += 1
        nc.gpsimd.sem_clear(range(first, stop))
    nc.all_engine_barrier()


def decoder_block(nc, x, g_mix, w_in, w_alpha_up, b_alpha, g_gla, w_conv, w_branch_a, w_branch_b, w_out,
                  g_ffn, w_router, b_router, w_gate_up, b_gate_up, w_down, b_down, g_final, out):
    y_conv = nc.dram_tensor("y_conv", (P, KT, S), F32, kind="Internal").ap()
    gates = nc.dram_tensor("gates", (P, 2 * KT, S), F32, kind="Internal").ap()
    h_rows = nc.dram_tensor("h_rows", (XROWS, D), F32, kind="Internal").ap()
    y_rows = nc.dram_tensor("y_rows", (XROWS, D), F32, kind="Internal").ap()

    with ExitStack() as whole:
        def sb(ctx, name, shape, dt=F32):
            return ctx.enter_context(nc.sbuf_tensor(name, shape, dt))

        cst = {"ident": sb(whole, "ident", [P, P]), "iota": sb(whole, "iota", [P, SUPER]),
               "tokens": sb(whole, "tokens", [P, TT, 3], BF16), "spare": sb(whole, "spare", [P, 2]),
               "eps": sb(whole, "eps", [P, 1]), "part": sb(whole, "part", [P, 1])}
        rank = sb(whole, "rank", [P, TT, E])
        gate3 = sb(whole, "gate3", [P, TT, E, 3], BF16)
        table = sb(whole, "table", [P, 4, W], I32)
        row0 = sb(whole, "row0", [P, W])

        with ExitStack() as mixer:
            cst["mask"] = sb(mixer, "mask", [P, P])
            cst["cumul"] = sb(mixer, "cumul", [P, P])
            cst["before"] = sb(mixer, "before", [P, P], BF16)
            cst["ones16"] = sb(mixer, "ones16", [P, P], BF16)
            constants(nc, sb, cst)
            with ExitStack() as upto_branches:
                v = sb(upto_branches, "v", [P, TT, V_W])
                with ExitStack() as projections:
                    h_hi = sb(projections, "h_hi", [P, KT, S], F32R)
                    h_lo = sb(projections, "h_lo", [P, KT, S], F32R)
                    inv_rms = sb(projections, "inv_rms", [P, TT, HEADS])
                    with ExitStack() as recurrence:
                        q, k = (sb(recurrence, "q", [P, HEADS, S]), sb(recurrence, "k", [P, HEADS, S]))
                        decay = sb(recurrence, "decay", [P, HEADS, S])
                        alpha_lr = k[0:RANK, 0]
                        norm_and_transpose(nc, x, g_mix, w_in, cst, h_hi, h_lo, alpha_lr, v)
                        project_qkv(nc, w_in, w_alpha_up, b_alpha, cst, h_hi, h_lo, alpha_lr, v, q, k, decay)
                        linear_attention(nc, g_gla, cst, v, q, k, decay, inv_rms)
                    project_rest(nc, w_in, w_conv, h_hi, h_lo, v, inv_rms, y_conv, gates)
                mix = sb(upto_branches, "mix", [P, KT, S])
                branch(nc, "b", w_branch_b, None, y_conv, gates[:, 0:KT, :], cst, mix)
                branch(nc, "a", w_branch_a, v, None, gates[:, KT:2 * KT, :], cst, mix)
                x2 = v
                project_out(nc, w_out, x, mix, x2)
                route(nc, x2, g_ffn, w_router, b_router, h_rows, y_rows, cst, rank, gate3, table, row0)
        clear_signals(nc)
        experts(nc, w_gate_up, b_gate_up, w_down, b_down, h_rows, y_rows, cst, rank, gate3, table, row0)
        finish(nc, y_rows, g_final, out, cst)


_INS = ["x", "g_mix", "w_in", "w_alpha_up", "b_alpha", "g_gla", "w_conv", "w_branch_a", "w_branch_b", "w_out",
        "g_ffn", "w_router", "b_router", "w_gate_up", "b_gate_up", "w_down", "b_down", "g_final"]


def kernel(**inputs):
    import concourse.bacc as bacc
    from concourse.bass_utils import run_bass_kernel_spmd

    nc = bacc.Bacc("TRN2", target_bir_lowering=False, num_devices=1)
    arrays, args = {}, []
    for name in _INS:
        a = np.ascontiguousarray(inputs[name])
        arrays[f"in_{name}"] = a
        t = nc.dram_tensor(f"in_{name}", a.shape, mybir.dt.from_np(a.dtype), kind="ExternalInput").ap()
        if name == "x":
            t = t.rearrange("b s d -> (b s) d")
        elif name == "g_gla":
            t = t.rearrange("l h v -> (l h v)")
        elif name == "g_final":
            pass
        elif len(a.shape) == 2:
            t = t.rearrange("l n -> (l n)")
        elif len(a.shape) == 3:
            t = t.rearrange("l a b -> (l a) b")
        else:
            t = t.rearrange("l e a b -> (l e) a b")
        args.append(t)
    out = nc.dram_tensor("out_0", (1, S, D), F32, kind="ExternalOutput").ap()
    decoder_block(nc, *args, out.rearrange("b s d -> (b s) d"))
    r = run_bass_kernel_spmd(nc, [arrays], core_ids=[0])
    return r.results[0]["out_0"]
```
